# Optimizing a Trainium2 kernel written in Bass

```python
import jax, jax.numpy as jnp
from jax import lax
import numpy as np

D_MODEL = 1024
BATCH = 1
SEQ = 1024
DEPTH = 2

N_MIXERS = 2
N_LRU_LAYERS = (DEPTH + 1) // 2
N_SB_LAYERS = DEPTH // 2
LRU_HEADS = max(4, D_MODEL // 64)
LRU_BLOCK = max(16, (((4 * D_MODEL) // 3) // LRU_HEADS) // 16 * 16)
LRU_WIDTH = LRU_HEADS * LRU_BLOCK
LRU_C = 8.0
CONV_WIDTH = 4
SB_HEAD_DIM = 64
SB_HEADS = max(4, D_MODEL // SB_HEAD_DIM)
SB_WIDTH = SB_HEADS * SB_HEAD_DIM
Q_BLOCK = 128
RMS_EPS = 1e-6

kernel_name = "hybrid_rglru_stickbreaking_trunk"

def rms_norm(x, g):
    xf = x.astype(jnp.float32)
    y = xf * lax.rsqrt(jnp.mean(xf * xf, axis=-1, keepdims=True) + RMS_EPS)
    return (y * g.astype(jnp.float32)).astype(x.dtype)

def causal_depthwise_conv(x, w, b):
    c = x.shape[-1]
    y = lax.conv_general_dilated(
        x, w[:, None, :].astype(x.dtype), window_strides=(1,),
        padding=[(CONV_WIDTH - 1, 0)], dimension_numbers=("NWC", "WIO", "NWC"),
        feature_group_count=c)
    return y + b.astype(x.dtype)

def _linear_recurrence_combine(left, right):
    a1, b1 = left
    a2, b2 = right
    return a1 * a2, a2 * b1 + b2

def rg_lru(x, w_gates, b_gates, lam):
    bsz, s, _ = x.shape
    xh = x.reshape(bsz, s, LRU_HEADS, LRU_BLOCK)
    gl = jnp.einsum("bshi,hio->bsho", xh, w_gates.astype(x.dtype)).astype(jnp.float32) + b_gates.astype(jnp.float32)
    r = jax.nn.sigmoid(gl[..., :LRU_BLOCK]).reshape(bsz, s, LRU_WIDTH)
    i = jax.nn.sigmoid(gl[..., LRU_BLOCK:]).reshape(bsz, s, LRU_WIDTH)
    log_a = LRU_C * r * jax.nn.log_sigmoid(lam.astype(jnp.float32))
    a = jnp.exp(log_a)
    mult = jnp.sqrt(-jnp.expm1(2.0 * log_a))
    bterm = mult * (i * x.astype(jnp.float32))
    _, h = lax.associative_scan(_linear_recurrence_combine, (a, bterm), axis=1)
    return h.astype(x.dtype)

def lru_mixer(h, w_in, conv_w, conv_b, w_gates, b_gates, lam, w_out):
    u = h @ w_in.astype(h.dtype)
    xb, gate = u[..., :LRU_WIDTH], u[..., LRU_WIDTH:]
    xb = causal_depthwise_conv(xb, conv_w, conv_b)
    y = rg_lru(xb, w_gates, b_gates, lam)
    return (y * jax.nn.silu(gate)) @ w_out.astype(h.dtype)

def stick_breaking_attention(q, k, v):
    s_len = q.shape[1]
    scale = SB_HEAD_DIM ** -0.5
    outs = []
    for qb in range(s_len // Q_BLOCK):
        t0 = qb * Q_BLOCK
        n_k = t0 + Q_BLOCK
        z = jnp.einsum("bthd,bshd->bhts", q[:, t0:n_k], k[:, :n_k]).astype(jnp.float32) * scale
        t_idx = t0 + jnp.arange(Q_BLOCK)[:, None]
        s_idx = jnp.arange(n_k)[None, :]
        causal = s_idx < t_idx
        log_beta = jax.nn.log_sigmoid(z)
        log_fail = jnp.where(causal, jax.nn.log_sigmoid(-z), 0.0)
        later = lax.cumsum(log_fail, axis=3, reverse=True) - log_fail
        att = jnp.where(causal, jnp.exp(log_beta + later), 0.0)
        outs.append(jnp.einsum("bhts,bshd->bthd", att.astype(v.dtype), v[:, :n_k]))
    return jnp.concatenate(outs, axis=1)

def sb_mixer(h, w_in, w_out):
    bsz, s, _ = h.shape
    u = h @ w_in.astype(h.dtype)
    q = u[..., :SB_WIDTH].reshape(bsz, s, SB_HEADS, SB_HEAD_DIM)
    k = u[..., SB_WIDTH:2 * SB_WIDTH].reshape(bsz, s, SB_HEADS, SB_HEAD_DIM)
    v = u[..., 2 * SB_WIDTH:3 * SB_WIDTH].reshape(bsz, s, SB_HEADS, SB_HEAD_DIM)
    gate = u[..., 3 * SB_WIDTH:]
    o = stick_breaking_attention(q, k, v).reshape(bsz, s, SB_WIDTH)
    return (o * jax.nn.silu(gate)) @ w_out.astype(h.dtype)

def setup_inputs(seed: int = 0) -> dict:
    key = jax.random.key(seed)
    ks = jax.random.split(key, 12)
    f32 = jnp.float32
    x = jax.random.normal(ks[0], (BATCH, SEQ, D_MODEL), f32)
    norm_g = 1.0 + 0.02 * jax.random.normal(ks[1], (DEPTH, D_MODEL), f32)
    final_norm_g = 1.0 + 0.02 * jax.random.normal(ks[2], (D_MODEL,), f32)
    lru_w_in = jax.random.normal(ks[3], (N_LRU_LAYERS, D_MODEL, 2 * LRU_WIDTH), f32) * D_MODEL ** -0.5
    lru_conv_w = jax.random.normal(ks[4], (N_LRU_LAYERS, CONV_WIDTH, LRU_WIDTH), f32) * CONV_WIDTH ** -0.5
    lru_conv_b = 0.01 * jax.random.normal(ks[5], (N_LRU_LAYERS, LRU_WIDTH), f32)
    lru_w_gates = jax.random.normal(ks[6], (N_LRU_LAYERS, LRU_HEADS, LRU_BLOCK, 2 * LRU_BLOCK), f32) * LRU_BLOCK ** -0.5
    lru_b_gates = 0.01 * jax.random.normal(ks[7], (N_LRU_LAYERS, LRU_HEADS, 2 * LRU_BLOCK), f32)
    u = jax.random.uniform(ks[8], (N_LRU_LAYERS, LRU_WIDTH), f32, minval=0.9, maxval=0.999)
    a0 = u ** (1.0 / LRU_C)
    lru_lambda = jnp.log(a0) - jnp.log1p(-a0)
    lru_w_out = jax.random.normal(ks[9], (N_LRU_LAYERS, LRU_WIDTH, D_MODEL), f32) * LRU_WIDTH ** -0.5
    sb_w_in = jax.random.normal(ks[10], (N_SB_LAYERS, D_MODEL, 4 * SB_WIDTH), f32) * D_MODEL ** -0.5
    sb_w_out = jax.random.normal(ks[11], (N_SB_LAYERS, SB_WIDTH, D_MODEL), f32) * SB_WIDTH ** -0.5
    return {"x": x, "norm_g": norm_g, "final_norm_g": final_norm_g,
            "lru_w_in": lru_w_in, "lru_conv_w": lru_conv_w, "lru_conv_b": lru_conv_b,
            "lru_w_gates": lru_w_gates, "lru_b_gates": lru_b_gates, "lru_lambda": lru_lambda,
            "lru_w_out": lru_w_out, "sb_w_in": sb_w_in, "sb_w_out": sb_w_out}

def reference(x, norm_g, final_norm_g, lru_w_in, lru_conv_w, lru_conv_b, lru_w_gates,
              lru_b_gates, lru_lambda, lru_w_out, sb_w_in, sb_w_out):
    for layer in range(DEPTH):
        h = rms_norm(x, norm_g[layer])
        j = layer // N_MIXERS
        if layer % N_MIXERS == 0:
            y = lru_mixer(h, lru_w_in[j], lru_conv_w[j], lru_conv_b[j], lru_w_gates[j],
                          lru_b_gates[j], lru_lambda[j], lru_w_out[j])
        else:
            y = sb_mixer(h, sb_w_in[j], sb_w_out[j])
        x = x + y
    return rms_norm(x, final_norm_g)


_drawn_inputs = setup_inputs


def setup_inputs(seed=0):
    import zlib

    import numpy as np

    out = dict(_drawn_inputs(seed))
    spreads = {}
    factors = {'norm_g': 3.594, 'final_norm_g': 2.784, 'lru_b_gates': 8.0}
    for name, (base, spread) in spreads.items():
        noise = np.random.default_rng([zlib.crc32(name.encode()), seed]).standard_normal(out[name].shape)
        drawn = base * np.exp(spread * noise) if base else spread * noise
        out[name] = __import__('jax').numpy.asarray(drawn.astype(out[name].dtype))
    for name, factor in factors.items():
        out[name] = (out[name] * factor).astype(out[name].dtype)
    return out
```

```python
import concourse.bass as bass
from concourse import mybir
from contextlib import ExitStack

P = 128
T = 1024
D = 1024
KD = D // P
HALF = 512
LRU = 1280
LT = LRU // P
GRP = 5
EPS = 1e-6
N_IN = 2 * LT
N_GATE = N_IN + 2 * KD
PAIRS = 8
HD = 64
N_QKV = N_GATE + PAIRS
N_OUT2 = N_QKV + 3 * PAIRS
N_ALL = N_OUT2 + KD
UNITS = 16
ROUNDS = 24
SCALE = HD ** -0.5
MASKED = -1e30
PAR_G, PAR_CW, PAR_CB, PAR_BR, PAR_BI, PAR_LAM, PAR_FG = 0, 16, 56, 66, 76, 86, 96
PAR = 104


def build(nc, xT, params, weights, w_gate, kept, out):
    F32, F32R, BF16 = mybir.dt.float32, mybir.dt.float32r, mybir.dt.bfloat16
    ALU, ACT = mybir.AluOpType, mybir.ActivationFunctionType

    ctx = ExitStack()
    with ctx:
        def sb(name, shape, dt=F32):
            return ctx.enter_context(nc.sbuf_tensor(name, shape, dt))

        def sem(name):
            return ctx.enter_context(nc.semaphore(name))

        class Count:
            def __init__(self, name, credit=0):
                self.sem, self.credit = sem(name), credit

            def after(self, t):
                return self.sem, t + 1 + self.credit

        split = sb("split", [P, 22 * T], F32R)
        h_hi, h_lo = split[:, 0:KD * T], split[:, KD * T:2 * KD * T]
        y_hi, y_lo = split[:, 0:LT * T], split[:, LT * T:2 * LT * T]
        xb_hi = split[:, 16 * T:19 * T]
        xb_lo = split[:, 19 * T:22 * T]
        rows = sb("rows", [P, LT * T])
        w_stage = sb("w_stage", [P, 2, D])
        w_hi = sb("w_hi", [P, 2, D], F32R)
        w_lo = sb("w_lo", [P, 2, D], F32R)
        par = sb("par", [P, PAR])
        tiny = sb("tiny", [P, 6, LT])
        ones = sb("ones", [P, 1])
        eps = sb("eps", [P, 1])
        zero = sb("zero", [P, 1])
        ident = sb("ident", [P, P])
        rstd = sb("rstd", [P, KD])
        ident_b = sb("ident_b", [P, P], BF16)
        mask = sb("mask", [P, P], BF16)
        with ExitStack() as turn:
            def tb(name, shape, dt=F32):
                return turn.enter_context(nc.sbuf_tensor(name, shape, dt))
            gw_stage = tb("gw_stage", [P, 3 * 256])
            gw_hi = tb("gw_hi", [P, 3 * 256], F32R)
            gw_lo = tb("gw_lo", [P, 3 * 256], F32R)
            taps = tb("taps", [P, T + 4])
            conv = tb("conv", [P, 3, T])
            gated = tb("gated", [P, 3, T])
            work = tb("work", [P, 4, T])
        with ExitStack() as turn:
            q_pair = tb("q_pair", [P, 2, 2, T], F32R)
            v_pair = tb("v_pair", [P, 2, KD, 2, P], F32R)
            att_hi = tb("att_hi", [P, KD, P], F32R)
            att_lo = tb("att_lo", [P, KD, P], F32R)
            fail = tb("fail", [P, 2, T + 1])
            vt = tb("vt", [P, T])
            o_part = tb("o_part", [P, HALF])
        with ExitStack() as turn:
            fin_sum = tb("fin_sum", [P, T])
            fin_sq = tb("fin_sq", [P, 2, T])
            fin_x = tb("fin_x", [P, 2, T])
            fin_out = tb("fin_out", [P, 4, T])
        k_pair = split[:, 16 * T:20 * T].rearrange("p (s h n) -> p s h n", s=2, h=2)
        k_low = split[:, 20 * T:22 * T].rearrange("p (s n) -> p s n", s=2)
        beta = rows[:, 8 * T:10 * T].rearrange("p (s n) -> p s n", s=2)
        sq_buf = {0: (gated[:, 2, :], gated), 1: (gated[:, 2, :], gated), 2: (fin_sum[:, :], fin_sq)}
        ps = [ctx.enter_context(nc.psum_tensor(f"ps{i}", [P, T], F32)) for i in range(4)]

        x_loaded = [sem(f"x_loaded{i}") for i in range(KD)]
        par_loaded, gw_loaded, stored = sem("par_loaded"), sem("gw_loaded"), sem("stored")
        w_loaded = [sem("w_loaded0"), sem("w_loaded1")]
        xs_loaded = [sem("xs_loaded0"), sem("xs_loaded1")]
        act_step, dve_step, pool_step, decay_ready, consts = (
            sem("act_step"), sem("dve_step"), sem("pool_step"), sem("decay_ready"), sem("consts"))
        w_hi_ready, w_lo_ready, w_used = Count("w_hi_ready"), Count("w_lo_ready"), Count("w_used", 2)
        gw_hi_ready, gw_lo_ready = Count("gw_hi_ready"), Count("gw_lo_ready", 1)
        sq_ready, sq_added = Count("sq_ready"), Count("sq_added")
        sums_done, root_done, rstd_ready, rstd_spread = Count("sums_done"), Count("root_done"), Count("rstd_ready"), Count("rstd_spread")
        hf_ready, hhi_ready, hlo_ready = Count("hf_ready"), Count("hhi_ready"), Count("hlo_ready")
        ri_done = Count("ri_done", 2)
        taps_ready, conv_done = Count("taps_ready", 1), Count("conv_done", 1)
        xbhi_ready, xblo_ready = Count("xbhi_ready"), Count("xblo_ready", 2)
        sg_ready, gated_done = Count("sg_ready"), Count("gated_done", 1)
        ri_sig, root_ready, lru_done = Count("ri_sig", 1), Count("root_ready"), Count("lru_done", 2)
        yhi_ready, ylo_ready = Count("yhi_ready"), Count("ylo_ready")
        x1_done = Count("x1_done", 2)
        x1_kept = sem("x1_kept")
        x1_loaded = [sem("x1_loaded0"), sem("x1_loaded1")]
        gsig_ready, silu_done = Count("gsig_ready"), Count("silu_done", 2)
        qhi_done, qlo_done = Count("qhi_done"), Count("qlo_done")
        khi_done, klo_done = Count("khi_done"), Count("klo_done")
        vt_done, vturn_done, vhi_done, vlo_done = Count("vt_done"), Count("vturn_done"), Count("vhi_done"), Count("vlo_done", 1)
        z_ready, sig_done, scan_done, att_done = Count("z_ready"), Count("sig_done"), Count("scan_done"), Count("att_done")
        turn_done, ahi_done, alo_done = Count("turn_done"), Count("ahi_done"), Count("alo_done", 2)
        av_done, opart_done, o_done = Count("av_done", 1), Count("opart_done"), Count("o_done", 2)
        ohi_ready, olo_ready = Count("ohi_ready"), Count("olo_ready")
        x2_done, fin_ready = Count("x2_done", 2), Count("fin_ready")
        fin_stored = [sem(f"fin_stored{i}") for i in range(4)]
        credited = [silu_done, vlo_done, alo_done, av_done, o_done, x2_done,
                    w_used, gw_lo_ready, ri_done, taps_ready, conv_done, xblo_ready, gated_done,
                    ri_sig, lru_done, x1_done]

        class Chain:
            def __init__(self, eng, s):
                self.eng, self.s, self.base, self.k = eng, s, 0, 0

            def __call__(self, ins):
                self.k += 1
                ins.then_inc(self.s, 1)
                self.eng.wait_ge(self.s, self.base + self.k)

            def enter(self, i, per):
                self.start, self.per = self.base + self.k, per
                self.base, self.k = self.start + i * per, 0

            def leave(self, trips):
                assert self.k == self.per, (self.k, self.per)
                self.base, self.k = self.start + trips * self.per, 0

        def at(t, n=T):
            return slice(t * n, t * n + n)

        def pv(base, t, n=1):
            return par[:, bass.ds(base + t, n)] if not isinstance(t, int) else par[:, base + t:base + t + n]

        def dram_tile(src, t):
            return src[bass.ds(t, 1)].rearrange("a p n -> p (a n)")

        def units(slot):
            r, out = 0, []
            for u in range(UNITS):
                h, b = divmod(u, KD)
                n = b // 4 + 1
                out.append((u, h, b, r, n))
                r += n
            return out
        PLAN = units(0)

        block = ctx.enter_context(nc.Block())

        @block.sync
        def _(sp):
            sp.dma_start(par[:, :], params).then_inc(par_loaded, 16)
            for k in range(KD):
                sp.dma_start(rows[:, at(k)], xT[k]).then_inc(x_loaded[k], 16)
            for m in range(2):
                sp.dma_start(w_stage[:, m, :], weights[m]).then_inc(w_loaded[m], 16)
            with sp.Fori(0, 2) as g:
                for j in range(GRP):
                    J = g * GRP + j
                    sp.wait_ge(*gw_lo_ready.after(J - 1))
                    sp.dma_start(gw_stage[:, :], dram_tile(w_gate, J)).then_inc(gw_loaded, 16)
                    for m in range(2):
                        sp.wait_ge(*w_lo_ready.after(J * 2 + m))
                        sp.dma_start(w_stage[:, m, :], dram_tile(weights, J * 2 + m + 2)).then_inc(w_loaded[m], 16)
            sp.wait_ge(*lru_done.after(LT - 1))
            with sp.Fori(0, KD // 2) as i:
                for q in range(2):
                    dt = i * 2 + q
                    sp.wait_ge(*x1_done.after(dt - 2))
                    sp.dma_start(work[:, q, :], dram_tile(xT, dt)).then_inc(xs_loaded[q], 16)
                    for m in range(2):
                        n = dt * 2 + m + N_IN
                        sp.wait_ge(*w_lo_ready.after(n))
                        sp.dma_start(w_stage[:, m, :], dram_tile(weights, n + 2)).then_inc(w_loaded[m], 16)
            with sp.Fori(0, KD) as k:
                sp.wait_ge(*x1_done.after(k))
                sp.dma_start(dram_tile(kept, k), rows[:, bass.ts(k, T)]).then_inc(x1_kept, 16)
            with sp.Fori(0, (N_OUT2 - N_GATE) // 2) as i:
                for m in range(2):
                    n = i * 2 + m + N_GATE
                    sp.wait_ge(*w_lo_ready.after(n))
                    sp.dma_start(w_stage[:, m, :], dram_tile(weights, n + 2)).then_inc(w_loaded[m], 16)
            sp.wait_ge(x1_kept, 16 * KD)
            sp.wait_ge(*olo_ready.after(PAIRS - 1))
            def last_loads(dt, q, more):
                sp.wait_ge(*x2_done.after(dt - 2))
                sp.dma_start(fin_x[:, q, :], dram_tile(kept, dt)).then_inc(x1_loaded[q], 16)
                if more:
                    sp.wait_ge(*w_lo_ready.after(dt + N_OUT2))
                    sp.dma_start(w_stage[:, q, :], dram_tile(weights, dt + N_OUT2 + 2)).then_inc(w_loaded[q], 16)
            with sp.Fori(0, KD // 2 - 1) as i:
                for q in range(2):
                    last_loads(i * 2 + q, q, True)
            for q in range(2):
                last_loads(KD - 2 + q, q, False)
            for k in range(KD):
                sp.wait_ge(*fin_ready.after(k))
                sp.dma_start(out[k], fin_out[:, k % 4, :]).then_inc(fin_stored[k % 4], 16)
            for b in range(4):
                sp.wait_ge(fin_stored[b], 16 * KD // 4)

        @block.gpsimd
        def _(pool):
            link = Chain(pool, pool_step)
            for c in credited:
                pool.sem_inc(c.sem, c.credit)
            nc.gpsimd.memset(ones[:, :], 1.0).then_inc(consts, 1)
            nc.gpsimd.memset(eps[:, :], EPS).then_inc(consts, 1)
            nc.gpsimd.memset(zero[:, :], 0.0).then_inc(consts, 1)
            nc.gpsimd.memset(taps[:, 0:4], 0.0).then_inc(consts, 1)
            link(nc.gpsimd.memset(ident[:, :], 0.0))
            nc.gpsimd.affine_select(out=ident[:, :], in_=ident[:, :], compare_op=ALU.not_equal, fill=1.0,
                                    base=0, pattern=[[-1, P]], channel_multiplier=1).then_inc(consts, 1)
            pool.wait_ge(consts, 5)
            nc.gpsimd.tensor_copy(ident_b[:, :], ident[:, :]).then_inc(consts, 1)
            link(nc.gpsimd.memset(mask[:, :], 0.0))
            nc.gpsimd.affine_select(out=mask[:, :], in_=mask[:, :], compare_op=ALU.is_ge, fill=MASKED,
                                    base=-1, pattern=[[-1, P]], channel_multiplier=1).then_inc(consts, 1)

            def weight_lo(n, m, width=D):
                pool.wait_ge(*w_hi_ready.after(n))
                pool.wait_ge(*w_used.after(n - 2))
                nc.gpsimd.tensor_tensor(w_lo[:, m, 0:width], w_stage[:, m, 0:width], w_hi[:, m, 0:width].bitcast(F32),
                                        ALU.subtract).then_inc(w_lo_ready.sem, 1)

            def h_low(base):
                for k in range(KD):
                    pool.wait_ge(*hhi_ready.after(base + k))
                    nc.gpsimd.tensor_tensor(h_lo[:, at(k)], work[:, k % 2, :], h_hi[:, at(k)].bitcast(F32),
                                            ALU.subtract).then_inc(hlo_ready.sem, 1)
            for m in range(2):
                weight_lo(m, m)
            h_low(0)
            with pool.Fori(0, 2) as g:
                for j in range(GRP):
                    J = g * GRP + j
                    weight_lo(J * 2 + 2, 0)
                    pool.wait_ge(*xbhi_ready.after(J))
                    nc.gpsimd.tensor_tensor(xb_lo[:, at(j % 3)], conv[:, j % 3, :], xb_hi[:, at(j % 3)].bitcast(F32),
                                            ALU.subtract).then_inc(xblo_ready.sem, 1)
                    pool.wait_ge(*gw_hi_ready.after(J))
                    pool.wait_ge(*ri_done.after(J - 1))
                    nc.gpsimd.tensor_tensor(gw_lo[:, :], gw_stage[:, :], gw_hi[:, :].bitcast(F32),
                                            ALU.subtract).then_inc(gw_lo_ready.sem, 1)
                    weight_lo(J * 2 + 3, 1)
            with pool.Fori(0, LT) as c:
                pool.wait_ge(*yhi_ready.after(c))
                nc.gpsimd.tensor_tensor(y_lo[:, bass.ts(c, T)], rows[:, bass.ts(c, T)], y_hi[:, bass.ts(c, T)].bitcast(F32),
                                        ALU.subtract).then_inc(ylo_ready.sem, 1)
            with pool.Fori(0, KD) as dt:
                for m in range(2):
                    weight_lo(dt * 2 + m + N_IN + 2, m)
            h_low(KD)
            with pool.Fori(0, PAIRS // 2) as i:
                for m in range(2):
                    weight_lo(i * 2 + m + N_GATE + 2, m)

            def attend(p, u):
                b = u % KD
                lo = T - (b + 1) * P
                pool.wait_ge(*scan_done.after(p * UNITS + u))
                nc.gpsimd.tensor_tensor(beta[:, u % 2, lo:T], beta[:, u % 2, lo:T], fail[:, u % 2, lo + 1:T + 1],
                                        ALU.mult).then_inc(att_done.sem, 1)

            def pair(i, s, more):
                p = i * 2 + s
                for u, h, b, r, n in PLAN:
                    if u + 1 < UNITS:
                        attend(p, u + 1)
                    elif more:
                        attend(p + 1, 0)
                    if more and u in (3, 7, 11):
                        c = 3 * s + u // 4 + N_QKV + 5
                        weight_lo(i * 6 + c, c % 2)
            for n in range(N_QKV + 2, N_QKV + 5):
                weight_lo(n, n % 2)
            attend(0, 0)
            with pool.Fori(0, PAIRS // 2 - 1) as i:
                for s in range(2):
                    pair(i, s, True)
            pair(PAIRS // 2 - 1, 0, True)
            pair(PAIRS // 2 - 1, 1, False)
            with pool.Fori(0, PAIRS) as p:
                pool.wait_ge(*ohi_ready.after(p))
                nc.gpsimd.tensor_tensor(h_lo[:, bass.ts(p, T)], rows[:, bass.ts(p, T)], h_hi[:, bass.ts(p, T)].bitcast(F32),
                                        ALU.subtract).then_inc(olo_ready.sem, 1)
            with pool.Fori(0, KD // 2 - 1) as i:
                for m in range(2):
                    weight_lo(i * 2 + m + N_OUT2 + 2, m)

        @block.scalar
        def _(act):
            link = Chain(act, act_step)

            def weight_hi(n, m, loads):
                act.wait_ge(w_loaded[m], loads * 16)
                act.wait_ge(*w_used.after(n - 2))
                nc.scalar.copy(w_hi[:, m, :], w_stage[:, m, :]).then_inc(w_hi_ready.sem, 1)

            def square(k, t):
                total, ring = sq_buf[t]
                if k >= 3:
                    act.wait_ge(*sq_added.after((KD - 1) * t + k - 3))
                dst = total if k == 0 else ring[:, k % 2, :]
                nc.scalar.activation(dst, rows[:, at(k)], ACT.Square).then_inc(sq_ready.sem, 1)

            def root(t):
                act.wait_ge(*sums_done.after(t))
                nc.scalar.activation(rstd[:, :], ps[3][:, 0:KD], ACT.Sqrt, bias=eps[:, :], scale=1.0 / D).then_inc(root_done.sem, 1)

            def h_high(base):
                for k in range(KD):
                    act.wait_ge(*hf_ready.after(base + k))
                    nc.scalar.copy(h_hi[:, at(k)], work[:, k % 2, :]).then_inc(hhi_ready.sem, 1)

            act.wait_ge(par_loaded, 16)
            lam = par[:, PAR_LAM:PAR_LAM + LT]
            link(nc.scalar.activation(tiny[:, 0, :], lam, ACT.Abs))
            nc.scalar.activation(tiny[:, 0, :], tiny[:, 0, :], ACT.Exp, scale=-1.0).then_inc(act_step, 1)
            link.k += 1
            for k in range(KD):
                act.wait_ge(x_loaded[k], 16)
                square(k, 0)
            act.wait_ge(consts, 5)
            for m in range(2):
                weight_hi(m, m, 1)
            root(0)
            h_high(0)

            def gates(J, j):
                act.wait_ge(*ri_done.after(J))
                act.wait_ge(*lru_done.after(J - 1))
                link(nc.scalar.activation(work[:, 0, :], ps[2][:, :], ACT.Sigmoid, bias=pv(PAR_BR, J)))
                link(nc.scalar.activation(work[:, 0, :], work[:, 0, :], ACT.Tanh, scale=tiny[:, 5, bass.ds(J, 1)]))
                nc.scalar.activation(work[:, 1, :], ps[3][:, :], ACT.Sigmoid, bias=pv(PAR_BI, J)).then_inc(ri_sig.sem, 1)
                nc.scalar.activation(work[:, 2, :], work[:, 0, :], ACT.Sqrt).then_inc(root_ready.sem, 1)

            act.wait_ge(decay_ready, 1)
            link_per = 2 * GRP
            with act.Fori(0, 2) as g:
                link.enter(g, link_per)
                for j in range(GRP):
                    J = g * GRP + j
                    act.wait_ge(*w_used.after(J * 2))
                    act.wait_ge(*conv_done.after(J - 1))
                    nc.scalar.copy(taps[:, 3:3 + T], ps[0][:, :]).then_inc(taps_ready.sem, 1)
                    weight_hi(J * 2 + 2, 0, J + 2)
                    act.wait_ge(*conv_done.after(J))
                    act.wait_ge(*ri_done.after(J - 1 if j == 0 else J - 2))
                    nc.scalar.copy(xb_hi[:, at(j % 3)], conv[:, j % 3, :]).then_inc(xbhi_ready.sem, 1)
                    act.wait_ge(*w_used.after(J * 2 + 1))
                    act.wait_ge(*lru_done.after(J - 2))
                    nc.scalar.activation(gated[:, j % 3, :], ps[1][:, :], ACT.Sigmoid).then_inc(sg_ready.sem, 1)
                    weight_hi(J * 2 + 3, 1, J + 2)
                    act.wait_ge(gw_loaded, (J + 1) * 16)
                    act.wait_ge(*ri_done.after(J - 1))
                    nc.scalar.copy(gw_hi[:, :], gw_stage[:, :]).then_inc(gw_hi_ready.sem, 1)
                    if j > 0:
                        gates(J - 1, j - 1)
                    if j == GRP - 1:
                        gates(J, j)
                link.leave(2)
            act.wait_ge(*ri_done.after(LT - 1))
            with act.Fori(0, LT) as c:
                act.wait_ge(*lru_done.after(c))
                nc.scalar.copy(y_hi[:, bass.ts(c, T)], rows[:, bass.ts(c, T)]).then_inc(yhi_ready.sem, 1)
            for dt in range(KD):
                for m in range(2):
                    weight_hi(dt * 2 + m + N_IN + 2, m, LT + 2 + dt)
                act.wait_ge(*x1_done.after(dt))
                square(dt, 1)
            root(1)
            h_high(KD)

            with act.Fori(0, PAIRS // 2) as i:
                for m in range(2):
                    p = i * 2 + m
                    act.wait_ge(*w_used.after(p + N_GATE))
                    act.wait_ge(*silu_done.after(p - 2))
                    nc.scalar.activation(beta[:, m, :], ps[m][:, :], ACT.Sigmoid).then_inc(gsig_ready.sem, 1)
                    weight_hi(p + N_GATE + 2, m, i + N_GATE // 2 + 2)

            def q_high(n, p, s):
                act.wait_ge(*w_used.after(n))
                for h in range(2):
                    own = slice(h * HD, h * HD + HD)
                    ins = nc.scalar.copy(q_pair[own, s, h, :], ps[0][own, :])
                ins.then_inc(qhi_done.sem, 1)

            def k_high(n, p, s):
                act.wait_ge(*w_used.after(n))
                for h in range(2):
                    own = slice(h * HD, h * HD + HD)
                    for dst in (own, slice(HD - h * HD, 2 * HD - h * HD)):
                        ins = nc.scalar.copy(k_pair[dst, s, h, :], ps[0][own, :])
                ins.then_inc(khi_done.sem, 1)

            def v_copy(n, p, s):
                act.wait_ge(*w_used.after(n))
                nc.scalar.copy(vt[:, :], ps[0][:, :]).then_inc(vt_done.sem, 1)

            def v_high(p, s):
                act.wait_ge(*vturn_done.after(p))
                nc.scalar.copy(v_pair[:, s, :, :, 0:HD], ps[0][:, :].rearrange("p (k h d) -> p k h d", k=KD, h=2)).then_inc(vhi_done.sem, 1)

            def sigmoids(p, u, free=True):
                lo = T - (u % KD + 1) * P
                U = p * UNITS + u
                act.wait_ge(*z_ready.after(U))
                if free:
                    act.wait_ge(*att_done.after(U - 2))
                    prev = PLAN[(u - 2) % UNITS]
                    act.wait_ge(*turn_done.after(p * ROUNDS + (prev[3] + prev[4] - 1 - (ROUNDS if u < 2 else 0))))
                nc.scalar.activation(fail[:, u % 2, lo:T], ps[1][:, lo:T], ACT.Sigmoid, scale=-SCALE)
                nc.scalar.activation(beta[:, u % 2, lo:T], ps[1][:, lo:T], ACT.Sigmoid, scale=SCALE).then_inc(sig_done.sem, 1)

            def pair(i, s, more):
                p = i * 2 + s
                for u, h, b, r, n in PLAN:
                    act.wait_ge(*av_done.after(p * UNITS + u - 1))
                    for x in range(n):
                        cnt = min(4, b + 1 - 4 * x)
                        bank = (r + x) % 2
                        act.wait_ge(*turn_done.after(p * ROUNDS + r + x))
                        nc.scalar.copy(att_hi[:, 4 * x:4 * x + cnt, :],
                                       ps[2][:, bank * HALF:bank * HALF + cnt * P].rearrange("p (k n) -> p k n", k=cnt)).then_inc(ahi_done.sem, 1)
                    if u + 2 < UNITS:
                        sigmoids(p, u + 2)
                    elif more:
                        sigmoids(p + 1, u + 2 - UNITS)
                    if more and u in (3, 7, 11):
                        c = 3 * s + u // 4 + N_QKV + 3
                        (q_high, k_high, v_copy)[u // 4](i * 6 + c, p + 1, 1 - s)
                        weight_hi(i * 6 + c + 2, c % 2, i * 3 + (c + 2) // 2 + 1)
                    if more and u == 13:
                        v_high(p + 1, 1 - s)
                    if u % 4 == 3:
                        B = p * 4 + u // 4
                        act.wait_ge(*av_done.after(p * UNITS + u))
                        act.wait_ge(*o_done.after(B - 1))
                        bank = (u // 4) % 2
                        nc.scalar.copy(o_part[h * HD:h * HD + HD, :], ps[3][HD:P, bank * HALF:bank * HALF + HALF]).then_inc(opart_done.sem, 1)

            q_high(N_QKV, 0, 0)
            weight_hi(N_QKV + 2, 0, (N_QKV + 2) // 2 + 1)
            k_high(N_QKV + 1, 0, 0)
            weight_hi(N_QKV + 3, 1, (N_QKV + 3) // 2 + 1)
            v_copy(N_QKV + 2, 0, 0)
            weight_hi(N_QKV + 4, 0, (N_QKV + 4) // 2 + 1)
            v_high(0, 0)
            sigmoids(0, 0, False)
            sigmoids(0, 1, False)
            with act.Fori(0, PAIRS // 2 - 1) as i:
                for s in range(2):
                    pair(i, s, True)
            pair(PAIRS // 2 - 1, 0, True)
            pair(PAIRS // 2 - 1, 1, False)

            act.wait_ge(*w_used.after(N_OUT2 - 1))
            with act.Fori(0, PAIRS) as p:
                act.wait_ge(*o_done.after(p * 4 + 3))
                nc.scalar.copy(h_hi[:, bass.ts(p, T)], rows[:, bass.ts(p, T)]).then_inc(ohi_ready.sem, 1)
            for dt in range(KD):
                if dt < KD - 2:
                    weight_hi(N_OUT2 + dt + 2, dt % 2, (N_OUT2 + dt + 2) // 2 + 1)
                act.wait_ge(*x2_done.after(dt))
                square(dt, 2)
            root(2)

        @block.vector
        def _(dve):
            link = Chain(dve, dve_step)
            dve.wait_ge(act_step, 2)
            e, s, s2, acc, z, kappa = (tiny[:, i, :] for i in range(6))
            link(nc.vector.tensor_scalar(s, e, 2.0, None, ALU.add))
            link(nc.vector.reciprocal(s, s))
            link(nc.vector.tensor_tensor(s, s, e, ALU.mult))
            link(nc.vector.tensor_tensor(s2, s, s, ALU.mult))
            link(nc.vector.tensor_scalar(acc, s2, 1.0 / 19, 1.0 / 17, ALU.mult, ALU.add))
            for d in (15, 13, 11, 9, 7, 5, 3, 1):
                link(nc.vector.tensor_tensor(acc, acc, s2, ALU.mult))
                link(nc.vector.tensor_scalar(acc, acc, 1.0 / d, None, ALU.add))
            link(nc.vector.tensor_tensor(acc, acc, s, ALU.mult))
            link(nc.vector.tensor_scalar(z, par[:, PAR_LAM:PAR_LAM + LT], -4.0, 0.0, ALU.mult, ALU.max))
            nc.vector.scalar_tensor_tensor(kappa, acc, 8.0, z, ALU.mult, ALU.add).then_inc(decay_ready, 1)

            def add_square(k, t):
                dve.wait_ge(*sq_ready.after(KD * t + k))
                if k > 1:
                    dve.wait_ge(*sq_added.after((KD - 1) * t + k - 2))
                total, ring = sq_buf[t]
                nc.vector.tensor_tensor(total, total, ring[:, k % 2, :], ALU.add).then_inc(sq_added.sem, 1)

            def normalise(t, gain, base):
                dve.wait_ge(*root_done.after(t))
                nc.vector.reciprocal(rstd[:, :], rstd[:, :]).then_inc(rstd_ready.sem, 1)
                dve.wait_ge(*rstd_spread.after(t))
                for k in range(KD):
                    if k > 1:
                        dve.wait_ge(*hlo_ready.after(base + k - 2))
                    nc.vector.scalar_tensor_tensor(work[:, k % 2, :], rows[:, at(k)], par[:, gain + k:gain + k + 1],
                                                   ps[2][:, :], ALU.mult, ALU.mult).then_inc(hf_ready.sem, 1)
            for k in range(1, KD):
                add_square(k, 0)
            normalise(0, PAR_G, 0)

            def recur(J, j):
                th, gi, rt, dn = (work[:, i, :] for i in range(4))
                dve.wait_ge(*ri_sig.after(J))
                link(nc.vector.tensor_scalar(dn, th, 1.0, None, ALU.add))
                link(nc.vector.reciprocal(dn, dn))
                dve.wait_ge(*root_ready.after(J))
                nc.vector.tensor_scalar(th, dn, 2.0, -1.0, ALU.mult, ALU.add)
                nc.vector.tensor_tensor(gi, gi, conv[:, j % 3, :], ALU.mult)
                link(nc.vector.scalar_tensor_tensor(rt, rt, 2.0, dn, ALU.mult, ALU.mult))
                link(nc.vector.tensor_tensor(rt, rt, gi, ALU.mult))
                link(nc.vector.tensor_tensor_scan(dn, th, rt, 0.0, ALU.mult, ALU.add))
                nc.vector.tensor_tensor(rows[:, bass.ts(J, T)], dn, gated[:, j % 3, :], ALU.mult).then_inc(lru_done.sem, 1)

            with dve.Fori(0, 2) as g:
                link.enter(g, GRP * 8)
                for j in range(GRP):
                    J = g * GRP + j
                    c = conv[:, j % 3, :]
                    dve.wait_ge(*taps_ready.after(J))
                    dve.wait_ge(*xblo_ready.after(J - 2))
                    link(nc.vector.tensor_scalar(c, taps[:, 3:3 + T], par[:, bass.ds(PAR_CW + 3 * LT + J, 1)],
                                                 par[:, bass.ds(PAR_CB + J, 1)], ALU.mult, ALU.add))
                    for tap in (2, 1, 0):
                        ins = nc.vector.scalar_tensor_tensor(c, taps[:, tap:tap + T], par[:, bass.ds(PAR_CW + tap * LT + J, 1)],
                                                             c, ALU.mult, ALU.add)
                        if tap:
                            link(ins)
                        else:
                            ins.then_inc(conv_done.sem, 1)
                    dve.wait_ge(*sg_ready.after(J))
                    nc.vector.tensor_tensor(gated[:, j % 3, :], ps[1][:, :], gated[:, j % 3, :], ALU.mult).then_inc(gated_done.sem, 1)
                    if j > 0:
                        recur(J - 1, j - 1)
                    if j == GRP - 1:
                        recur(J, j)
                link.leave(2)
            dve.wait_ge(*ylo_ready.after(LT - 1))
            for dt in range(KD):
                dve.wait_ge(*w_used.after(N_IN + 2 * dt + 1))
                dve.wait_ge(xs_loaded[dt % 2], 16 * (dt // 2 + 1))
                nc.vector.tensor_tensor(rows[:, at(dt)], ps[dt % 2][:, :], work[:, dt % 2, :], ALU.add).then_inc(x1_done.sem, 1)
                if dt:
                    add_square(dt, 1)
            normalise(1, PAR_G + KD, KD)

            dve.wait_ge(*hlo_ready.after(2 * KD - 1))
            link(nc.vector.memset(fail[:, :, T:T + 1], 1.0))
            dve.wait_ge(x1_kept, 16 * KD)
            with dve.Fori(0, PAIRS // 2) as i:
                for m in range(2):
                    p = i * 2 + m
                    dve.wait_ge(*gsig_ready.after(p))
                    nc.vector.tensor_tensor(rows[:, bass.ts(p, T)], ps[m][:, :], beta[:, m, :], ALU.mult).then_inc(silu_done.sem, 1)

            def q_low(p, s):
                dve.wait_ge(*qhi_done.after(p))
                for h in range(2):
                    own, other = slice(h * HD, h * HD + HD), slice(HD - h * HD, 2 * HD - h * HD)
                    ins = nc.vector.tensor_tensor(q_pair[other, s, h, :], ps[0][own, :], q_pair[own, s, h, :].bitcast(F32), ALU.subtract)
                ins.then_inc(qlo_done.sem, 1)

            def k_lo(p, s):
                dve.wait_ge(*khi_done.after(p))
                for h in range(2):
                    own = slice(h * HD, h * HD + HD)
                    ins = nc.vector.tensor_tensor(k_low[own, s, :], ps[0][own, :], k_pair[own, s, h, :].bitcast(F32), ALU.subtract)
                ins.then_inc(klo_done.sem, 1)

            def v_low(p, s):
                dve.wait_ge(*vhi_done.after(p))
                nc.vector.tensor_tensor(v_pair[:, s, :, :, HD:P], ps[0][:, :].rearrange("p (k h d) -> p k h d", k=KD, h=2),
                                        v_pair[:, s, :, :, 0:HD].bitcast(F32), ALU.subtract).then_inc(vlo_done.sem, 1)

            def products(p, u):
                lo = T - (u % KD + 1) * P
                dve.wait_ge(*sig_done.after(p * UNITS + u))
                keys = fail[:, u % 2, lo:T][:, ::-1]
                nc.vector.tensor_tensor_scan(keys, keys, zero[:, :].to_broadcast([P, T - lo]), 1.0, ALU.mult, ALU.add).then_inc(scan_done.sem, 1)

            def pair(i, s, more):
                p = i * 2 + s
                for u, h, b, r, n in PLAN:
                    if u + 1 < UNITS:
                        products(p, u + 1)
                    elif more:
                        products(p + 1, 0)
                    for x in range(n):
                        cnt = min(4, b + 1 - 4 * x)
                        bank = (r + x) % 2
                        dve.wait_ge(*ahi_done.after(p * ROUNDS + r + x))
                        nc.vector.tensor_tensor(att_lo[:, 4 * x:4 * x + cnt, :],
                                                ps[2][:, bank * HALF:bank * HALF + cnt * P].rearrange("p (k n) -> p k n", k=cnt),
                                                att_hi[:, 4 * x:4 * x + cnt, :].bitcast(F32), ALU.subtract).then_inc(alo_done.sem, 1)
                    if more and u == 3:
                        q_low(p + 1, 1 - s)
                    if more and u == 7:
                        k_lo(p + 1, 1 - s)
                    if more and u == 13:
                        v_low(p + 1, 1 - s)
                    if u % 4 == 3:
                        B = p * 4 + u // 4
                        bank = (u // 4) % 2
                        own = slice(h * HD, h * HD + HD)
                        cols = bass.ds(p * T + (b // 4) * HALF, HALF)
                        dve.wait_ge(*opart_done.after(B))
                        link(nc.vector.tensor_tensor(o_part[own, :], ps[3][0:HD, bank * HALF:bank * HALF + HALF], o_part[own, :], ALU.add))
                        nc.vector.tensor_tensor(rows[own, cols], rows[own, cols], o_part[own, :], ALU.mult).then_inc(o_done.sem, 1)

            q_low(0, 0)
            k_lo(0, 0)
            v_low(0, 0)
            products(0, 0)
            with dve.Fori(0, PAIRS // 2 - 1) as i:
                link.enter(i, 8)
                for s in range(2):
                    pair(i, s, True)
                link.leave(PAIRS // 2 - 1)
            pair(PAIRS // 2 - 1, 0, True)
            pair(PAIRS // 2 - 1, 1, False)

            dve.wait_ge(*olo_ready.after(PAIRS - 1))
            for dt in range(KD):
                dve.wait_ge(*w_used.after(N_OUT2 + dt))
                dve.wait_ge(x1_loaded[dt % 2], 16 * (dt // 2 + 1))
                nc.vector.tensor_tensor(rows[:, at(dt)], ps[dt % 2][:, :], fin_x[:, dt % 2, :], ALU.add).then_inc(x2_done.sem, 1)
                if dt:
                    add_square(dt, 2)
            dve.wait_ge(*root_done.after(2))
            nc.vector.reciprocal(rstd[:, :], rstd[:, :]).then_inc(rstd_ready.sem, 1)
            dve.wait_ge(*rstd_spread.after(2))
            for k in range(KD):
                if k > 3:
                    dve.wait_ge(fin_stored[k % 4], 16)
                nc.vector.scalar_tensor_tensor(fin_out[:, k % 4, :], rows[:, at(k)], par[:, PAR_FG + k:PAR_FG + k + 1],
                                               ps[2][:, :], ALU.mult, ALU.mult).then_inc(fin_ready.sem, 1)

        @block.tensor
        def _(pe):
            def sums(t, ready):
                pe.wait_ge(*ready)
                total = sq_buf[t][0]
                for k in range(KD):
                    ins = nc.tensor.matmul(ps[3][:, k:k + 1], total[:, at(k, P)], ones[:, :], start=True, stop=True)
                ins.then_inc(sums_done.sem, 1)
                pe.wait_ge(*rstd_ready.after(t))
                for k in range(KD):
                    ins = nc.tensor.matmul(ps[2][:, at(k, P)], rstd[:, k:k + 1].to_broadcast([P, P]), ident[:, :],
                                           start=True, stop=True)
                ins.then_inc(rstd_spread.sem, 1)

            def tile_product(dst, wh, wl, mh, ml, c, first, last):
                for s in range(2):
                    cols = slice(s * HALF, s * HALF + HALF)
                    nc.tensor.matmul(dst[:, cols], wh, mh[:, c * T + s * HALF:c * T + s * HALF + HALF], start=first, stop=False)
                    nc.tensor.matmul(dst[:, cols], wh, ml[:, c * T + s * HALF:c * T + s * HALF + HALF], start=False, stop=False)
                for s in range(2):
                    cols = slice(s * HALF, s * HALF + HALF)
                    ins = nc.tensor.matmul(dst[:, cols], wl, mh[:, c * T + s * HALF:c * T + s * HALF + HALF], start=False, stop=last)
                return ins

            pe.wait_ge(consts, 5)
            sums(0, sq_added.after(6))

            def project(n, m, dst, first_ever=False):
                pe.wait_ge(*w_lo_ready.after(n))
                for c in range(KD):
                    if first_ever:
                        pe.wait_ge(*hlo_ready.after(c))
                    ins = tile_product(dst, w_hi[:, m, at(c, P)], w_lo[:, m, at(c, P)], h_hi, h_lo, c, c == 0, c == KD - 1)
                ins.then_inc(w_used.sem, 1)

            with pe.Fori(0, 2) as g:
                for j in range(GRP):
                    J = g * GRP + j

                    def gate_products(J, j):
                        pe.wait_ge(*gw_lo_ready.after(J))
                        pe.wait_ge(*ri_sig.after(J - 1))
                        if j < GRP - 1:
                            pe.wait_ge(*xblo_ready.after(J + 1))
                        else:
                            pe.wait_ge(*xblo_ready.after(J))
                        slots = [s for s in range(3) if 0 <= j - 1 + s < GRP]
                        for s in slots:
                            src = (j - 1 + s) % 3
                            for o in range(2):
                                w = slice(s * 256 + o * P, s * 256 + o * P + P)
                                ins = tile_product(ps[2 + o], gw_hi[:, w], gw_lo[:, w], xb_hi, xb_lo, src, s == slots[0], s == slots[-1])
                        ins.then_inc(ri_done.sem, 1)

                    pe.wait_ge(*taps_ready.after(J - 1))
                    project(J * 2, 0, ps[0], j == 0)
                    pe.wait_ge(*gated_done.after(J - 1))
                    project(J * 2 + 1, 1, ps[1])
                    if j > 0:
                        gate_products(J - 1, j - 1)
                    if j == GRP - 1:
                        gate_products(J, j)
            with pe.Fori(0, KD // 2) as i:
                for q in range(2):
                    dt = i * 2 + q
                    pe.wait_ge(*x1_done.after(dt - 2))
                    for m in range(2):
                        n = dt * 2 + m + N_IN
                        pe.wait_ge(*w_lo_ready.after(n))
                        for c5 in range(GRP):
                            c = m * GRP + c5
                            if q == 0:
                                pe.wait_ge(*ylo_ready.after(c))
                            ins = tile_product(ps[q], w_hi[:, m, at(c5, P)], w_lo[:, m, at(c5, P)], y_hi, y_lo, c, c == 0, c == LT - 1)
                        ins.then_inc(w_used.sem, 1)
            sums(1, sq_added.after(13))

            pe.wait_ge(*hlo_ready.after(2 * KD - 1))
            with pe.Fori(0, PAIRS // 2) as i:
                for m in range(2):
                    pe.wait_ge(*silu_done.after(i * 2 + m - 2))
                    project(i * 2 + m + N_GATE, m, ps[m])

            def turn_v(p):
                pe.wait_ge(*vt_done.after(p))
                for k in range(KD):
                    ins = nc.tensor.transpose(ps[0][:, at(k, P)], vt[:, at(k, P)], ident[:, :])
                ins.then_inc(vturn_done.sem, 1)

            def project_slice(i, s, u):
                kind, quarter = divmod(u, 4)
                p = i * 2 + s + 1
                c = 3 * s + 3 + kind + N_QKV
                n, m = i * 6 + c, c % 2
                if quarter == 0:
                    pe.wait_ge(*w_lo_ready.after(n))
                    if kind == 0:
                        pe.wait_ge(*vlo_done.after(p - 1))
                    if kind == 1:
                        pe.wait_ge(*qlo_done.after(p))
                    if kind == 2:
                        pe.wait_ge(*klo_done.after(p))
                for ch in (2 * quarter, 2 * quarter + 1):
                    ins = tile_product(ps[0], w_hi[:, m, at(ch, P)], w_lo[:, m, at(ch, P)], h_hi, h_lo, ch, ch == 0, ch == KD - 1)
                if quarter == 3:
                    ins.then_inc(w_used.sem, 1)

            def scores(p, s, u):
                h, b = divmod(u, KD)
                lo = T - (b + 1) * P
                own, blk = slice(h * HD, h * HD + HD), at(b, P)
                for a, e in ((max(lo, HALF), T), (lo, HALF)):
                    if a >= e:
                        continue
                    keys = slice(a - lo, e - lo)
                    last = e < T
                    nc.tensor.matmul(ps[1][:, a:e], q_pair[:, s, h, blk], k_pair[:, s, h, keys], start=True, stop=False)
                    ins = nc.tensor.matmul(ps[1][:, a:e], q_pair[own, s, h, blk], k_low[own, s, keys], start=False, stop=last)
                    if not last:
                        ins = nc.tensor.matmul(ps[1][:, T - P:T], ident_b[:, :], mask[:, :], start=False, stop=True)
                ins.then_inc(z_ready.sem, 1)

            def turn(p, u, h, b, r, n):
                pe.wait_ge(*att_done.after(p * UNITS + u))
                lo = T - (b + 1) * P
                for x in range(n):
                    bank = (r + x) % 2
                    pe.wait_ge(*alo_done.after(p * ROUNDS + r + x - 2))
                    for y in range(4 * x, min(4 * x + 4, b + 1)):
                        ins = nc.tensor.transpose(ps[2][:, bank * HALF + (y % 4) * P:bank * HALF + (y % 4) * P + P],
                                                  beta[:, u % 2, lo + y * P:lo + y * P + P], ident[:, :])
                    ins.then_inc(turn_done.sem, 1)

            def values(p, s, u, h, b, r, n):
                bank = (u // 4) % 2
                if u % 4 == 0:
                    pe.wait_ge(*o_done.after(p * 4 + u // 4 - 2))
                dst = ps[3][:, bank * HALF + (b % 4) * P:bank * HALF + (b % 4) * P + P]
                for x in range(n):
                    pe.wait_ge(*alo_done.after(p * ROUNDS + r + x))
                    for y in range(4 * x, min(4 * x + 4, b + 1)):
                        nc.tensor.matmul(dst, v_pair[:, s, y, h, :], att_hi[:, y, :], start=y == 0, stop=False)
                        ins = nc.tensor.matmul(dst, v_pair[:, s, y, h, :], att_lo[:, y, :], start=False, stop=y == b)
                ins.then_inc(av_done.sem, 1)

            def pair(i, s, more):
                p = i * 2 + s
                for u, h, b, r, n in PLAN:
                    if u + 2 < UNITS or more:
                        pe.wait_ge(*sig_done.after(p * UNITS + u + 1))
                        if u + 2 < UNITS:
                            scores(p, s, u + 2)
                        else:
                            scores(p + 1, 1 - s, u + 2 - UNITS)
                    turn(p, u, h, b, r, n)
                    if more and u < 12:
                        project_slice(i, s, u)
                    if more and u == 13:
                        turn_v(p + 1)
                    values(p, s, u, h, b, r, n)

            pe.wait_ge(*silu_done.after(PAIRS - 2))
            project(N_QKV, 0, ps[0])
            pe.wait_ge(*qlo_done.after(0))
            project(N_QKV + 1, 1, ps[0])
            pe.wait_ge(*klo_done.after(0))
            project(N_QKV + 2, 0, ps[0])
            turn_v(0)
            pe.wait_ge(*silu_done.after(PAIRS - 1))
            scores(0, 0, 0)
            pe.wait_ge(*sig_done.after(0))
            scores(0, 0, 1)
            pe.wait_ge(*vlo_done.after(0))
            with pe.Fori(0, PAIRS // 2 - 1) as i:
                for s in range(2):
                    pair(i, s, True)
            pair(PAIRS // 2 - 1, 0, True)
            pair(PAIRS // 2 - 1, 1, False)

            pe.wait_ge(*sig_done.after(PAIRS * UNITS - 1))
            for c in range(PAIRS):
                pe.wait_ge(*olo_ready.after(c))
            with pe.Fori(0, KD // 2) as i:
                for q in range(2):
                    pe.wait_ge(*x2_done.after(i * 2 + q - 2))
                    project(i * 2 + q + N_OUT2, q, ps[q])
            sums(2, sq_added.after(20))


def kernel(**inputs):
    import numpy as np
    import concourse.bacc as bacc
    from concourse.bass_utils import run_bass_kernel_spmd

    a = {k: np.asarray(v) for k, v in inputs.items()}

    def cols(v):
        return v.reshape(-1, P).T

    heads, blk = a["lru_w_gates"].shape[1], a["lru_w_gates"].shape[2]
    bg = a["lru_b_gates"][0]
    params = np.concatenate(
        [cols(a["norm_g"][0]), cols(a["norm_g"][1])] + [cols(a["lru_conv_w"][0, t]) for t in range(4)]
        + [cols(a["lru_conv_b"][0]), cols(np.ascontiguousarray(bg[:, :blk]).reshape(-1)),
           cols(np.ascontiguousarray(bg[:, blk:]).reshape(-1)), cols(a["lru_lambda"][0]), cols(a["final_norm_g"])], axis=1)
    full = np.zeros((2, LRU, LRU), np.float32)
    for h in range(heads):
        s = slice(h * blk, h * blk + blk)
        full[0, s, s] = a["lru_w_gates"][0, h, :, :blk]
        full[1, s, s] = a["lru_w_gates"][0, h, :, blk:]
    w_gate = np.zeros((LT, P, 3, 2, P), np.float32)
    for t in range(LT):
        for s in range(3):
            if 0 <= t - 1 + s < LT:
                w_gate[t, :, s] = full[:, (t - 1 + s) * P:(t + s) * P, t * P:(t + 1) * P].transpose(1, 0, 2)
    w_gate = w_gate.reshape(LT, P, 3 * 256)

    def tiles(w, chunks):
        k, n = w.shape
        return w.reshape(k // (P * chunks), chunks, P, n // P, P).transpose(3, 0, 2, 1, 4).reshape(n // P, -1, P, chunks * P)

    wi = tiles(a["lru_w_in"][0], KD)[:, 0]
    wi = np.stack([wi[:LT], wi[LT:]], axis=1).reshape(N_IN, P, D)
    wo = tiles(a["lru_w_out"][0], GRP).reshape(2 * KD, P, GRP * P)
    wo = np.concatenate([wo, np.zeros((2 * KD, P, D - GRP * P), np.float32)], axis=2)
    sbw = tiles(a["sb_w_in"][0], KD)[:, 0].reshape(4, KD, P, D).transpose(1, 0, 2, 3).reshape(4 * KD, P, D)
    sbo = tiles(a["sb_w_out"][0], KD)[:, 0]
    weights = np.concatenate([wi, wo, sbw[3::4], sbw.reshape(KD, 4, P, D)[:, :3].reshape(3 * KD, P, D), sbo], axis=0)
    host = {"xT": np.ascontiguousarray(a["x"][0].T).reshape(KD, P, T), "params": params, "weights": weights, "w_gate": w_gate}

    nc = bacc.Bacc("TRN2", target_bir_lowering=False, num_devices=1)
    arrays, args = {}, []
    for name, v in host.items():
        v = np.ascontiguousarray(v)
        arrays[f"in_{name}"] = v
        args.append(nc.dram_tensor(f"in_{name}", v.shape, mybir.dt.from_np(v.dtype), kind="ExternalInput").ap())
    out = nc.dram_tensor("out_dram", (KD, P, T), mybir.dt.float32, kind="ExternalOutput").ap()
    kept = nc.dram_tensor("kept_x1", (KD, P, T), mybir.dt.float32, kind="Internal").ap()
    build(nc, *args, kept, out)
    r = run_bass_kernel_spmd(nc, [arrays], core_ids=[0])
    return r.results[0]["out_dram"].reshape(D, T).T.reshape(1, T, D)
```

```python
import concourse.bass as bass
from concourse import mybir
from contextlib import ExitStack

P = 128
T = 1024
D = 1024
KD = D // P
HALF = 512
LRU = 1280
LT = LRU // P
GRP = 5
EPS = 1e-6
N_IN = 2 * LT
N_GATE = N_IN + 2 * KD
PAIRS = 8
HD = 64
N_QKV = N_GATE + PAIRS
N_OUT2 = N_QKV + 3 * PAIRS
N_ALL = N_OUT2 + KD
UNITS = 16
ROUNDS = 24
SCALE = HD ** -0.5
MASKED = -1e30
PAR_G, PAR_CW, PAR_CB, PAR_BR, PAR_BI, PAR_LAM, PAR_FG = 0, 16, 56, 66, 76, 86, 96
PAR = 104


def build(nc, xT, params, weights, w_gate, kept, out):
    F32, F32R, BF16 = mybir.dt.float32, mybir.dt.float32r, mybir.dt.bfloat16
    ALU, ACT = mybir.AluOpType, mybir.ActivationFunctionType

    ctx = ExitStack()
    with ctx:
        def sb(name, shape, dt=F32):
            return ctx.enter_context(nc.sbuf_tensor(name, shape, dt))

        def sem(name):
            return ctx.enter_context(nc.semaphore(name))

        class Count:
            def __init__(self, name, credit=0):
                self.sem, self.credit = sem(name), credit

            def after(self, t):
                return self.sem, t + 1 + self.credit

        split = sb("split", [P, 22 * T], F32R)
        h_hi, h_lo = split[:, 0:KD * T], split[:, KD * T:2 * KD * T]
        xb_hi, xb_lo = split[:, 16 * T:19 * T], split[:, 19 * T:22 * T]
        rows = sb("rows", [P, LT * T])
        w_stage = sb("w_stage", [P, D])
        w_hi = sb("w_hi", [P, 2, D], F32R)
        w_lo = sb("w_lo", [P, 2, D], F32R)
        scale = sb("scale", [P, T])
        par = sb("par", [P, PAR])
        tiny = sb("tiny", [P, 7, LT])
        ones = sb("ones", [P, 1])
        eps = sb("eps", [P, 1])
        zero = sb("zero", [P, 1])
        ident = sb("ident", [P, P])
        rstd = sb("rstd", [P, KD])
        ident_b = sb("ident_b", [P, P], BF16)
        mask = sb("mask", [P, P], BF16)
        with ExitStack() as turn:
            def tb(name, shape, dt=F32):
                return turn.enter_context(nc.sbuf_tensor(name, shape, dt))
            gw_stage = tb("gw_stage", [P, 3 * 256])
            gw_hi = tb("gw_hi", [P, 3 * 256], F32R)
            gw_lo = tb("gw_lo", [P, 3 * 256], F32R)
            taps = tb("taps", [P, T + 4])
            conv = tb("conv", [P, 3, T])
            gated = tb("gated", [P, 3, T])
            work = tb("work", [P, 4, T])
        with ExitStack() as turn:
            q_pair = tb("q_pair", [P, 2, 2, T], F32R)
            v_pair = tb("v_pair", [P, 2, KD, 2, P], F32R)
            att = tb("att", [P, KD, 2, P], F32R)
            fail = tb("fail", [P, 2, T + 1])
            proj = tb("proj", [P, T])
            o_part = tb("o_part", [P, 2, P])
        with ExitStack() as turn:
            fin_sum = tb("fin_sum", [P, T])
            fin_sq = tb("fin_sq", [P, 2, T])
            fin_x = tb("fin_x", [P, 2, T])
            fin_out = tb("fin_out", [P, KD, T])
        k_pair = split[:, 16 * T:20 * T].rearrange("p (s h n) -> p s h n", s=2, h=2)
        k_low = split[:, 20 * T:22 * T].rearrange("p (s n) -> p s n", s=2)
        beta = rows[:, 8 * T:10 * T].rearrange("p (s n) -> p s n", s=2)
        sq_buf = {0: (gated[:, 2, :], gated), 1: (gated[:, 2, :], gated), 2: (fin_sum[:, :], fin_sq)}
        ps = [ctx.enter_context(nc.psum_tensor(f"ps{i}", [P, T], F32)) for i in range(4)]

        x_loaded = [sem(f"x_loaded{i}") for i in range(KD)]
        par_loaded, w_loaded, gw_loaded, x1_kept = sem("par_loaded"), sem("w_loaded"), sem("gw_loaded"), sem("x1_kept")
        xs_loaded = [sem("xs_loaded0"), sem("xs_loaded1")]
        x1_loaded = [sem("x1_loaded0"), sem("x1_loaded1")]
        stored = sem("stored")
        act_step, dve_step, pool_step, decay_ready, consts = (
            sem("act_step"), sem("dve_step"), sem("pool_step"), sem("decay_ready"), sem("consts"))
        w_hi_ready, w_lo_ready, w_used = Count("w_hi_ready"), Count("w_lo_ready"), Count("w_used", 2)
        gw_hi_ready, gw_lo_ready = Count("gw_hi_ready"), Count("gw_lo_ready", 1)
        sq_ready, sq_added = Count("sq_ready"), Count("sq_added")
        sums_done, root_done, rstd_ready, rstd_spread, scale_ready = (
            Count("sums_done"), Count("root_done"), Count("rstd_ready"), Count("rstd_spread"), Count("scale_ready"))
        hhi_ready, hlo_ready = Count("hhi_ready"), Count("hlo_ready")
        taps_ready, conv_done = Count("taps_ready", 1), Count("conv_done", 1)
        xbhi_ready, xblo_ready = Count("xbhi_ready"), Count("xblo_ready", 2)
        gated_done, gsig_done, gsilu_done = Count("gated_done", 1), Count("gsig_done"), Count("gsilu_done")
        ri_done, ri_sig, root_ready, lru_done = Count("ri_done", 2), Count("ri_sig", 1), Count("root_ready"), Count("lru_done", 2)
        yhi_act, yhi_pool, ylo_pool, ylo_dve = Count("yhi_act"), Count("yhi_pool"), Count("ylo_pool"), Count("ylo_dve")
        x1_done = Count("x1_done", 2)
        pg_done, bsig_done, silu_done = Count("pg_done", 2), Count("bsig_done"), Count("silu_done", 2)
        proj_done = Count("proj_done")
        qhi_done, qlo_done = Count("qhi_done"), Count("qlo_done")
        khi_done, klo_done, kdup_done = Count("khi_done"), Count("klo_done"), Count("kdup_done")
        vturn_done, vhi_done, vlo_done = Count("vturn_done"), Count("vhi_done"), Count("vlo_done")
        z_ready, sig_done, scan_done, att_done = Count("z_ready"), Count("sig_done"), Count("scan_done"), Count("att_done")
        turn_done, ahi_done, alo_done = Count("turn_done"), Count("ahi_done"), Count("alo_done", 2)
        av_done, opart_done, o_done = Count("av_done", 1), Count("opart_done"), Count("o_done", 2)
        ohi_ready, olo_ready = Count("ohi_ready"), Count("olo_ready")
        x2_done, gain_done, fin_dve, fin_pool = Count("x2_done", 2), Count("gain_done"), Count("fin_dve"), Count("fin_pool")
        credited = [w_used, gw_lo_ready, taps_ready, conv_done, xblo_ready, gated_done, ri_done, ri_sig, lru_done,
                    x1_done, pg_done, silu_done, alo_done, av_done, o_done, x2_done]

        class Chain:
            def __init__(self, eng, s):
                self.eng, self.s, self.base, self.k = eng, s, 0, 0

            def __call__(self, ins):
                self.k += 1
                ins.then_inc(self.s, 1)
                self.eng.wait_ge(self.s, self.base + self.k)

            def enter(self, i, per):
                self.start, self.per = self.base + self.k, per
                self.base, self.k = self.start + i * per, 0

            def leave(self, trips):
                assert self.k == self.per, (self.k, self.per)
                self.base, self.k = self.start + trips * self.per, 0

        def at(t, n=T):
            return slice(t * n, t * n + n)

        def dram_tile(src, t):
            return src[bass.ds(t, 1)].rearrange("a p n -> p (a n)")

        def y_col(c):
            return (c * T, (KD + c) * T) if c < KD else ((8 + c) * T, (10 + c) * T)

        PLAN, r = [], 0
        for u in range(UNITS):
            h, b = divmod(u, KD)
            b = KD - 1 - b if h else b
            PLAN.append((u, h, b, r, b // 4 + 1))
            r += b // 4 + 1
        assert r == ROUNDS
        FILL = [1, 1, 2, 2, 2, 2, 2, 2, 2, 2, 2, 2, 2, 0, 0, 0]
        assert sum(FILL) == 3 * KD
        Q_AT, K_AT, V_AT = 4, 8, 12
        W_HI_AT = (Q_AT + 1, K_AT + 1, V_AT + 1)
        W_LO_AT = (Q_AT + 1, K_AT + 1, V_AT + 2), (Q_AT + 2, K_AT + 2, V_AT + 3)
        OUT_AT = 3

        def left(u):
            return T - (PLAN[u % UNITS][2] + 1) * P

        block = ctx.enter_context(nc.Block())

        @block.sync
        def _(sp):
            def load_weights(n):
                sp.wait_ge(*w_lo_ready.after(n - 1))
                sp.dma_start(w_stage[:, :], dram_tile(weights, n)).then_inc(w_loaded, 16)

            sp.dma_start(par[:, :], params).then_inc(par_loaded, 16)
            for k in range(KD):
                sp.dma_start(rows[:, at(k)], xT[k]).then_inc(x_loaded[k], 16)
                if k == 1:
                    sp.dma_start(w_stage[:, :], weights[0]).then_inc(w_loaded, 16)
            load_weights(1)
            with sp.Fori(0, 2) as g:
                for j in range(GRP):
                    J = g * GRP + j
                    sp.wait_ge(*gw_lo_ready.after(J - 1))
                    sp.dma_start(gw_stage[:, :], dram_tile(w_gate, J)).then_inc(gw_loaded, 16)
                    for m in range(2):
                        load_weights(J * 2 + m + 2)
            sp.wait_ge(*lru_done.after(LT - 1))
            with sp.Fori(0, KD // 2) as i:
                for q in range(2):
                    dt = i * 2 + q
                    sp.wait_ge(*x1_done.after(dt - 2))
                    sp.dma_start(work[:, q, :], dram_tile(xT, dt)).then_inc(xs_loaded[q], 16)
                    for m in range(2):
                        load_weights(dt * 2 + m + N_IN + 2)
            with sp.Fori(0, KD) as k:
                sp.wait_ge(*x1_done.after(k))
                sp.dma_start(dram_tile(kept, k), rows[:, bass.ts(k, T)]).then_inc(x1_kept, 16)
            with sp.Fori(N_GATE + 2, N_OUT2 + 2) as n:
                load_weights(n)
            sp.wait_ge(x1_kept, 16 * KD)
            sp.wait_ge(*olo_ready.after(PAIRS - 1))

            def last_loads(dt, q, more):
                sp.wait_ge(*x2_done.after(dt - 2))
                sp.dma_start(fin_x[:, q, :], dram_tile(kept, dt)).then_inc(x1_loaded[q], 16)
                if more:
                    load_weights(dt + N_OUT2 + 2)
            with sp.Fori(0, KD // 2 - 1) as i:
                for q in range(2):
                    last_loads(i * 2 + q, q, True)
            for q in range(2):
                last_loads(KD - 2 + q, q, False)
            for k in range(KD):
                sp.wait_ge(*(fin_pool.after(k // 4) if k % 4 == 3 else fin_dve.after(k - k // 4)))
                sp.dma_start(out[k], fin_out[:, k, :]).then_inc(stored, 16)
            sp.wait_ge(stored, 16 * KD)

        @block.gpsimd
        def _(pool):
            link = Chain(pool, pool_step)
            for c in credited:
                pool.sem_inc(c.sem, c.credit)
            nc.gpsimd.memset(ones[:, :], 1.0).then_inc(consts, 1)
            nc.gpsimd.memset(eps[:, :], EPS).then_inc(consts, 1)
            nc.gpsimd.memset(zero[:, :], 0.0).then_inc(consts, 1)
            nc.gpsimd.memset(taps[:, 0:4], 0.0).then_inc(consts, 1)
            link(nc.gpsimd.memset(ident[:, :], 0.0))
            nc.gpsimd.affine_select(out=ident[:, :], in_=ident[:, :], compare_op=ALU.not_equal, fill=1.0,
                                    base=0, pattern=[[-1, P]], channel_multiplier=1).then_inc(consts, 1)
            pool.wait_ge(consts, 5)
            nc.gpsimd.tensor_copy(ident_b[:, :], ident[:, :]).then_inc(consts, 1)
            link(nc.gpsimd.memset(mask[:, :], 0.0))
            nc.gpsimd.affine_select(out=mask[:, :], in_=mask[:, :], compare_op=ALU.is_ge, fill=MASKED,
                                    base=-1, pattern=[[-1, P]], channel_multiplier=1).then_inc(consts, 1)

            def low(dst, src, hi):
                return nc.gpsimd.tensor_tensor(dst, src, hi.bitcast(F32), ALU.subtract)

            def weight_lo(n, m):
                pool.wait_ge(*w_hi_ready.after(n))
                low(w_lo[:, m, :], w_stage[:, :], w_hi[:, m, :]).then_inc(w_lo_ready.sem, 1)

            for n in range(2):
                weight_lo(n, n)
            with pool.Fori(0, 2) as g:
                for j in range(GRP):
                    J = g * GRP + j
                    weight_lo(J * 2 + 2, 0)
                    pool.wait_ge(*xbhi_ready.after(J))
                    low(xb_lo[:, at(j % 3)], conv[:, j % 3, :], xb_hi[:, at(j % 3)]).then_inc(xblo_ready.sem, 1)
                    pool.wait_ge(*gsig_done.after(J))
                    nc.gpsimd.tensor_tensor(gated[:, j % 3, :], gated[:, j % 3, :], rows[:, bass.ts(J, T)],
                                            ALU.mult).then_inc(gsilu_done.sem, 1)
                    weight_lo(J * 2 + 3, 1)
                    pool.wait_ge(*gw_hi_ready.after(J))
                    low(gw_lo[:, :], gw_stage[:, :], gw_hi[:, :]).then_inc(gw_lo_ready.sem, 1)
            pool.wait_ge(*w_used.after(N_IN - 1))
            for c in range(9):
                hi, lo = y_col(c)
                if c < 7:
                    pool.wait_ge(*lru_done.after(c))
                    nc.gpsimd.tensor_copy(split[:, hi:hi + T], rows[:, at(c)]).then_inc(yhi_pool.sem, 1)
                    pool.wait_ge(*yhi_pool.after(c))
                else:
                    pool.wait_ge(*yhi_act.after(c - 7))
                low(split[:, lo:lo + T], rows[:, at(c)], split[:, hi:hi + T]).then_inc(ylo_pool.sem, 1)
            with pool.Fori(N_IN // 2 + 1, N_GATE // 2 + 1) as i:
                for m in range(2):
                    weight_lo(i * 2 + m, m)

            def silu(p, m):
                pool.wait_ge(*bsig_done.after(p))
                nc.gpsimd.tensor_tensor(rows[:, at(p) if isinstance(p, int) else bass.ts(p, T)],
                                        rows[:, at(p) if isinstance(p, int) else bass.ts(p, T)], beta[:, m, :],
                                        ALU.mult).then_inc(silu_done.sem, 1)
            weight_lo(N_GATE + 2, 0)
            weight_lo(N_GATE + 3, 1)
            silu(0, 0)
            silu(1, 1)
            with pool.Fori(1, PAIRS // 2) as i:
                for m in range(2):
                    silu(i * 2 + m, m)
                    weight_lo(i * 2 + m + N_GATE + 2, m)

            def k_lower(p, s, h):
                pool.wait_ge(*khi_done.after(p))
                own = slice(h * HD, h * HD + HD)
                low(k_low[own, s, :], proj[own, :], k_pair[own, s, h, :]).then_inc(klo_done.sem, 1)
                pool.wait_ge(*klo_done.after(2 * p + h))

            def weight_lo_half(n, m, half):
                if half == 0:
                    pool.wait_ge(*w_hi_ready.after(n))
                ins = low(w_lo[:, m, at(half, HALF)], w_stage[:, at(half, HALF)], w_hi[:, m, at(half, HALF)])
                if half == 1:
                    ins.then_inc(w_lo_ready.sem, 1)

            def attend(p, u):
                lo = left(u)
                pool.wait_ge(*scan_done.after(p * UNITS + u))
                nc.gpsimd.tensor_tensor(beta[:, u % 2, lo:T], beta[:, u % 2, lo:T], fail[:, u % 2, lo + 1:T + 1],
                                        ALU.mult).then_inc(att_done.sem, 1)

            def o_lower(p):
                pool.wait_ge(*ohi_ready.after(p))
                low(h_lo[:, at(p)], rows[:, at(p)], h_hi[:, at(p)]).then_inc(olo_ready.sem, 1)

            def pair(i, s, more):
                p = i * 2 + s
                for u in range(UNITS):
                    if u + 1 < UNITS:
                        attend(p, u + 1)
                    elif more:
                        attend(p + 1, 0)
                    if more and u in (K_AT + 3, K_AT + 4):
                        pool.wait_ge(*att_done.after(p * UNITS + u + 1))
                        k_lower(p + 1, 1 - s, u - K_AT - 3)
                    for half in range(2):
                        if more and u in W_LO_AT[half]:
                            c = 3 * s + W_LO_AT[half].index(u) + N_QKV + 5
                            weight_lo_half(i * 6 + c, c % 2, half)
                    if not more and u < PAIRS - 1:
                        o_lower(u)
            weight_lo(N_QKV + 2, 0)
            pool.wait_ge(*w_lo_ready.after(N_QKV + 2))
            k_lower(0, 0, 0)
            k_lower(0, 0, 1)
            for n in range(N_QKV + 3, N_QKV + 5):
                weight_lo(n, n % 2)
            attend(0, 0)
            with pool.Fori(0, PAIRS // 2 - 1) as i:
                for s in range(2):
                    pair(i, s, True)
            pair(PAIRS // 2 - 1, 0, True)
            pair(PAIRS // 2 - 1, 1, False)
            o_lower(PAIRS - 1)
            with pool.Fori(0, KD // 2 - 1) as i:
                for m in range(2):
                    weight_lo(i * 2 + m + N_OUT2 + 2, m)
            pool.wait_ge(*scale_ready.after(2))
            pool.wait_ge(*gain_done.after(KD - 1))
            for k in (3, 7):
                nc.gpsimd.tensor_tensor(fin_out[:, k, :], rows[:, at(k)], scale[:, :], ALU.mult).then_inc(fin_pool.sem, 1)

        @block.scalar
        def _(act):
            link = Chain(act, act_step)

            def weight_hi(n, m):
                act.wait_ge(w_loaded, (n + 1) * 16)
                act.wait_ge(*w_used.after(n - 2))
                nc.scalar.copy(w_hi[:, m, :], w_stage[:, :]).then_inc(w_hi_ready.sem, 1)

            def square(k, t):
                total, ring = sq_buf[t]
                if k >= 3:
                    act.wait_ge(*sq_added.after((KD - 1) * t + k - 3))
                dst = total if k == 0 else ring[:, k % 2, :]
                nc.scalar.activation(dst, rows[:, at(k)], ACT.Square).then_inc(sq_ready.sem, 1)

            def h_high(k, gain):
                nc.scalar.activation(h_hi[:, at(k)], rows[:, at(k)], ACT.Copy, scale=par[:, gain + k:gain + k + 1]).then_inc(hhi_ready.sem, 1)

            def root(t):
                act.wait_ge(*sums_done.after(t))
                nc.scalar.activation(rstd[:, :], ps[3][:, 0:KD], ACT.Sqrt, bias=eps[:, :], scale=1.0 / D).then_inc(root_done.sem, 1)

            def keep_scale(t):
                act.wait_ge(*rstd_spread.after(t))
                nc.scalar.copy(scale[:, :], ps[2][:, :]).then_inc(scale_ready.sem, 1)

            act.wait_ge(par_loaded, 16)
            link(nc.scalar.activation(tiny[:, 0, :], par[:, PAR_LAM:PAR_LAM + LT], ACT.Abs))
            link(nc.scalar.activation(tiny[:, 0, :], tiny[:, 0, :], ACT.Exp, scale=-1.0))
            for k in range(KD):
                act.wait_ge(x_loaded[k], 16)
                square(k, 0)
                h_high(k, PAR_G)
                if k == 3:
                    weight_hi(0, 0)
            act.wait_ge(consts, 5)
            root(0)
            weight_hi(1, 1)
            keep_scale(0)

            def gates(J, j):
                act.wait_ge(*ri_done.after(J))
                act.wait_ge(*lru_done.after(J - 1))
                nc.scalar.activation(work[:, 1, :], ps[3][:, :], ACT.Sigmoid, bias=par[:, bass.ds(PAR_BI + J, 1)])
                ins = nc.scalar.activation(work[:, 0, :], ps[2][:, :], ACT.Sigmoid, bias=par[:, bass.ds(PAR_BR + J, 1)])
                ins.then_inc(ri_sig.sem, 1)
                act.wait_ge(*ri_sig.after(J))
                nc.scalar.activation(work[:, 3, :], work[:, 0, :], ACT.Exp, scale=tiny[:, 6, bass.ds(J, 1)])
                link(nc.scalar.activation(work[:, 0, :], work[:, 0, :], ACT.Tanh, scale=tiny[:, 5, bass.ds(J, 1)]))
                nc.scalar.activation(work[:, 2, :], work[:, 0, :], ACT.Sqrt).then_inc(root_ready.sem, 1)

            act.wait_ge(decay_ready, 1)
            with act.Fori(0, 2) as g:
                link.enter(g, GRP)
                for j in range(GRP):
                    J = g * GRP + j
                    weight_hi(J * 2 + 2, 0)
                    act.wait_ge(*conv_done.after(J))
                    act.wait_ge(*ri_done.after(J - 1 if j == 0 else J - 2))
                    nc.scalar.copy(xb_hi[:, at(j % 3)], conv[:, j % 3, :]).then_inc(xbhi_ready.sem, 1)
                    act.wait_ge(*gated_done.after(J))
                    nc.scalar.activation(rows[:, bass.ts(J, T)], gated[:, j % 3, :], ACT.Sigmoid).then_inc(gsig_done.sem, 1)
                    weight_hi(J * 2 + 3, 1)
                    act.wait_ge(gw_loaded, (J + 1) * 16)
                    act.wait_ge(*ri_done.after(J - 1))
                    nc.scalar.copy(gw_hi[:, :], gw_stage[:, :]).then_inc(gw_hi_ready.sem, 1)
                    if j > 0:
                        gates(J - 1, j - 1)
                    if j == GRP - 1:
                        gates(J, j)
                link.leave(2)
            for c in range(7, LT):
                act.wait_ge(*lru_done.after(c))
                hi, lo = y_col(c)
                nc.scalar.copy(split[:, hi:hi + T], rows[:, at(c)]).then_inc(yhi_act.sem, 1)
            for i in range(KD // 2):
                n = N_IN + 4 * i + 2
                for q in range(2):
                    weight_hi(n + 2 * q, 0)
                    if q == 0:
                        weight_hi(n + 1, 1)
                    act.wait_ge(*x1_done.after(2 * i + q))
                    square(2 * i + q, 1)
                weight_hi(n + 3, 1)

            act.wait_ge(*w_used.after(N_GATE - 1))
            for k in range(KD):
                h_high(k, PAR_G + KD)
            weight_hi(N_GATE + 2, 0)
            root(1)
            weight_hi(N_GATE + 3, 1)
            keep_scale(1)

            def gate_sigmoid(p, m):
                act.wait_ge(*pg_done.after(p))
                act.wait_ge(*silu_done.after(p - 2))
                nc.scalar.activation(beta[:, m, :], rows[:, at(p) if isinstance(p, int) else bass.ts(p, T)], ACT.Sigmoid).then_inc(bsig_done.sem, 1)
            gate_sigmoid(0, 0)
            gate_sigmoid(1, 1)
            with act.Fori(1, PAIRS // 2) as i:
                for m in range(2):
                    gate_sigmoid(i * 2 + m, m)
                    weight_hi(i * 2 + m + N_GATE + 2, m)

            def q_high(p, s):
                act.wait_ge(*proj_done.after(p * 3))
                for h in range(2):
                    own = slice(h * HD, h * HD + HD)
                    ins = nc.scalar.copy(q_pair[own, s, h, :], proj[own, :])
                ins.then_inc(qhi_done.sem, 1)

            def k_high(p, s):
                act.wait_ge(*proj_done.after(p * 3 + 1))
                for h in range(2):
                    own = slice(h * HD, h * HD + HD)
                    ins = nc.scalar.copy(k_pair[own, s, h, :], proj[own, :])
                ins.then_inc(khi_done.sem, 1)

            def v_high(p, s):
                act.wait_ge(*vturn_done.after(p))
                nc.scalar.copy(v_pair[:, s, :, :, 0:HD], ps[0][:, :].rearrange("p (k h d) -> p k h d", k=KD, h=2)).then_inc(vhi_done.sem, 1)

            def sigmoids(p, u, free=True):
                lo = left(u)
                U = p * UNITS + u
                act.wait_ge(*z_ready.after(U))
                if free:
                    prev = PLAN[(u - 2) % UNITS]
                    act.wait_ge(*att_done.after(U - 2))
                    act.wait_ge(*turn_done.after(p * ROUNDS + (prev[3] + prev[4] - 1 - (ROUNDS if u < 2 else 0))))
                nc.scalar.activation(fail[:, u % 2, lo:T], ps[1][:, lo:T], ACT.Sigmoid, scale=-SCALE)
                nc.scalar.activation(beta[:, u % 2, lo:T], ps[1][:, lo:T], ACT.Sigmoid, scale=SCALE).then_inc(sig_done.sem, 1)

            def o_second(p, k):
                h, bank = k // 4, k % 2
                act.wait_ge(*av_done.after(p * UNITS + 2 * k + 1))
                act.wait_ge(*o_done.after(p * KD + k - 1))
                nc.scalar.copy(o_part[h * HD:h * HD + HD, :, :],
                               ps[3][HD:P, at(bank, HALF)].rearrange("p (u x n) -> p u x n", u=2, x=2)[:, :, 0, :]).then_inc(opart_done.sem, 1)

            def o_high(p):
                act.wait_ge(*o_done.after(p * KD + KD - 1))
                nc.scalar.copy(h_hi[:, at(p)], rows[:, at(p)]).then_inc(ohi_ready.sem, 1)

            def pair(i, s, more):
                p = i * 2 + s
                for u, h, b, r, n in PLAN:
                    act.wait_ge(*av_done.after(p * UNITS + u - 1))
                    for x in range(n):
                        cnt, bank = min(4, b + 1 - 4 * x), (r + x) % 2
                        act.wait_ge(*turn_done.after(p * ROUNDS + r + x))
                        nc.scalar.copy(att[:, 4 * x:4 * x + cnt, 0, :],
                                       ps[2][:, bank * HALF:bank * HALF + cnt * P].rearrange("p (k n) -> p k n", k=cnt)).then_inc(ahi_done.sem, 1)
                    if u + 2 < UNITS:
                        sigmoids(p, u + 2)
                    elif more:
                        sigmoids(p + 1, u + 2 - UNITS)
                    if u % 2 == 0 and u > 0:
                        o_second(p, u // 2 - 1)
                    if more and u == Q_AT + 1:
                        q_high(p + 1, 1 - s)
                    if more and u == K_AT + 1:
                        k_high(p + 1, 1 - s)
                    if more and u in W_HI_AT:
                        c = 3 * s + W_HI_AT.index(u) + N_QKV + 5
                        weight_hi(i * 6 + c, c % 2)
                    if more and u == V_AT + 2:
                        v_high(p + 1, 1 - s)
                    if u == UNITS - 1:
                        o_second(p, KD - 1)
                    if not more and u < PAIRS - 1:
                        if u == 0:
                            act.wait_ge(*w_used.after(N_OUT2 - 1))
                        o_high(u)

            q_high(0, 0)
            weight_hi(N_QKV + 2, 0)
            k_high(0, 0)
            weight_hi(N_QKV + 3, 1)
            weight_hi(N_QKV + 4, 0)
            v_high(0, 0)
            sigmoids(0, 0, False)
            sigmoids(0, 1, False)
            with act.Fori(0, PAIRS // 2 - 1) as i:
                for s in range(2):
                    pair(i, s, True)
            pair(PAIRS // 2 - 1, 0, True)
            pair(PAIRS // 2 - 1, 1, False)
            o_high(PAIRS - 1)

            for dt in range(KD):
                if dt < KD - 2:
                    weight_hi(N_OUT2 + dt + 2, dt % 2)
                act.wait_ge(*x2_done.after(dt))
                square(dt, 2)
                nc.scalar.activation(rows[:, at(dt)], rows[:, at(dt)], ACT.Copy, scale=par[:, PAR_FG + dt:PAR_FG + dt + 1]).then_inc(gain_done.sem, 1)
            root(2)
            keep_scale(2)

        @block.vector
        def _(dve):
            link = Chain(dve, dve_step)
            dve.wait_ge(act_step, 2)
            e, s_, s2, acc, z, kappa, kappa2 = (tiny[:, i, :] for i in range(7))
            link(nc.vector.tensor_scalar(s_, e, 2.0, None, ALU.add))
            link(nc.vector.reciprocal(s_, s_))
            link(nc.vector.tensor_tensor(s_, s_, e, ALU.mult))
            link(nc.vector.tensor_tensor(s2, s_, s_, ALU.mult))
            link(nc.vector.tensor_scalar(acc, s2, 1.0 / 19, 1.0 / 17, ALU.mult, ALU.add))
            for d in (15, 13, 11, 9, 7, 5, 3, 1):
                link(nc.vector.tensor_tensor(acc, acc, s2, ALU.mult))
                link(nc.vector.tensor_scalar(acc, acc, 1.0 / d, None, ALU.add))
            link(nc.vector.tensor_tensor(acc, acc, s_, ALU.mult))
            link(nc.vector.tensor_scalar(z, par[:, PAR_LAM:PAR_LAM + LT], -4.0, 0.0, ALU.mult, ALU.max))
            link(nc.vector.scalar_tensor_tensor(kappa, acc, 8.0, z, ALU.mult, ALU.add))
            nc.vector.tensor_scalar(kappa2, kappa, -2.0, None, ALU.mult).then_inc(decay_ready, 1)

            def low(dst, src, hi):
                return nc.vector.tensor_tensor(dst, src, hi.bitcast(F32), ALU.subtract)

            def add_square(k, t):
                dve.wait_ge(*sq_ready.after(KD * t + k))
                if k > 1:
                    dve.wait_ge(*sq_added.after((KD - 1) * t + k - 2))
                total, ring = sq_buf[t]
                nc.vector.tensor_tensor(total, total, ring[:, k % 2, :], ALU.add).then_inc(sq_added.sem, 1)

            def h_lower(k, gain, t):
                dve.wait_ge(*hhi_ready.after(KD * t + k))
                nc.vector.scalar_tensor_tensor(h_lo[:, at(k)], rows[:, at(k)], par[:, gain + k:gain + k + 1],
                                               h_hi[:, at(k)].bitcast(F32), ALU.mult, ALU.subtract).then_inc(hlo_ready.sem, 1)

            def invert(t):
                dve.wait_ge(*root_done.after(t))
                nc.vector.reciprocal(rstd[:, :], rstd[:, :]).then_inc(rstd_ready.sem, 1)

            for k in range(KD):
                if k:
                    add_square(k, 0)
                h_lower(k, PAR_G, 0)
            invert(0)

            def recur(J, j):
                th, gi, rt, a = (work[:, i, :] for i in range(4))
                dve.wait_ge(*root_ready.after(J))
                link(nc.vector.scalar_tensor_tensor(a, a, 1.0, th, ALU.add, ALU.mult))
                nc.vector.tensor_tensor(gi, gi, conv[:, j % 3, :], ALU.mult)
                link(nc.vector.tensor_scalar(a, a, -1.0, 1.0, ALU.mult, ALU.add))
                link(nc.vector.scalar_tensor_tensor(rt, a, 1.0, rt, ALU.add, ALU.mult))
                link(nc.vector.tensor_tensor(rt, rt, gi, ALU.mult))
                link(nc.vector.tensor_tensor_scan(th, a, rt, 0.0, ALU.mult, ALU.add))
                dve.wait_ge(*gsilu_done.after(J))
                nc.vector.tensor_tensor(rows[:, bass.ts(J, T)], th, gated[:, j % 3, :], ALU.mult).then_inc(lru_done.sem, 1)

            dve.wait_ge(*scale_ready.after(0))
            dve.wait_ge(consts, 5)
            with dve.Fori(0, 2) as g:
                link.enter(g, GRP * 8)
                for j in range(GRP):
                    J = g * GRP + j
                    c = conv[:, j % 3, :]
                    dve.wait_ge(*w_used.after(J * 2))
                    dve.wait_ge(*conv_done.after(J - 1))
                    ins = nc.vector.tensor_tensor(taps[:, 3:3 + T], ps[0][:, :], scale[:, :], ALU.mult)
                    ins.then_inc(taps_ready.sem, 1)
                    dve.wait_ge(*taps_ready.after(J))
                    dve.wait_ge(*xblo_ready.after(J - 2))
                    link(nc.vector.tensor_scalar(c, taps[:, 3:3 + T], par[:, bass.ds(PAR_CW + 3 * LT + J, 1)],
                                                 par[:, bass.ds(PAR_CB + J, 1)], ALU.mult, ALU.add))
                    for tap in (2, 1, 0):
                        ins = nc.vector.scalar_tensor_tensor(c, taps[:, tap:tap + T], par[:, bass.ds(PAR_CW + tap * LT + J, 1)],
                                                             c, ALU.mult, ALU.add)
                        if tap:
                            link(ins)
                        else:
                            ins.then_inc(conv_done.sem, 1)
                    dve.wait_ge(*w_used.after(J * 2 + 1))
                    nc.vector.tensor_tensor(gated[:, j % 3, :], ps[1][:, :], scale[:, :], ALU.mult).then_inc(gated_done.sem, 1)
                    if j > 0:
                        recur(J - 1, j - 1)
                    if j == GRP - 1:
                        recur(J, j)
                link.leave(2)
            dve.wait_ge(*yhi_act.after(2))
            hi, lo = y_col(LT - 1)
            low(split[:, lo:lo + T], rows[:, at(LT - 1)], split[:, hi:hi + T]).then_inc(ylo_dve.sem, 1)
            dve.wait_ge(*ylo_pool.after(LT - 2))
            dve.wait_ge(*ylo_dve.after(0))
            for dt in range(KD):
                i, q = divmod(dt, 2)
                dve.wait_ge(*w_used.after(N_IN + 4 * i + 2 + q))
                dve.wait_ge(xs_loaded[q], 16 * (i + 1))
                nc.vector.tensor_tensor(rows[:, at(dt)], ps[q][:, :], work[:, q, :], ALU.add).then_inc(x1_done.sem, 1)
                if dt:
                    add_square(dt, 1)
            for k in range(KD):
                h_lower(k, PAR_G + KD, 1)

            invert(1)
            link(nc.vector.memset(fail[:, :, T:T + 1], 1.0))
            dve.wait_ge(x1_kept, 16 * KD)
            dve.wait_ge(*scale_ready.after(1))
            with dve.Fori(0, PAIRS // 2) as i:
                for m in range(2):
                    p = i * 2 + m
                    dve.wait_ge(*w_used.after(p + N_GATE))
                    nc.vector.tensor_tensor(rows[:, bass.ts(p, T)], ps[m][:, :], scale[:, :], ALU.mult).then_inc(pg_done.sem, 1)

            def scaled(n):
                dve.wait_ge(*w_used.after(n))
                nc.vector.tensor_tensor(proj[:, :], ps[0][:, :], scale[:, :], ALU.mult).then_inc(proj_done.sem, 1)

            def q_low(p, s):
                dve.wait_ge(*qhi_done.after(p))
                for h in range(2):
                    own, other = slice(h * HD, h * HD + HD), slice(HD - h * HD, 2 * HD - h * HD)
                    ins = low(q_pair[other, s, h, :], proj[own, :], q_pair[own, s, h, :])
                ins.then_inc(qlo_done.sem, 1)

            def k_double(p, s):
                dve.wait_ge(*khi_done.after(p))
                for h in range(2):
                    own, other = slice(h * HD, h * HD + HD), slice(HD - h * HD, 2 * HD - h * HD)
                    ins = nc.vector.tensor_copy(k_pair[other, s, h, :], k_pair[own, s, h, :].bitcast(F32))
                ins.then_inc(kdup_done.sem, 1)

            def v_low(p, s):
                dve.wait_ge(*vhi_done.after(p))
                low(v_pair[:, s, :, :, HD:P], ps[0][:, :].rearrange("p (k h d) -> p k h d", k=KD, h=2),
                    v_pair[:, s, :, :, 0:HD]).then_inc(vlo_done.sem, 1)

            def products(p, u):
                lo = left(u)
                dve.wait_ge(*sig_done.after(p * UNITS + u))
                keys = fail[:, u % 2, lo:T][:, ::-1]
                nc.vector.tensor_tensor_scan(keys, keys, zero[:, :].to_broadcast([P, T - lo]), 1.0, ALU.mult, ALU.add).then_inc(scan_done.sem, 1)

            def o_join(p, k):
                h, bank = k // 4, k % 2
                own = slice(h * HD, h * HD + HD)
                v_hi = ps[3][0:HD, at(bank, HALF)].rearrange("p (u x n) -> p u x n", u=2, x=2)
                part = o_part[own, :, :]
                dve.wait_ge(*opart_done.after(p * KD + k))
                link(nc.vector.tensor_tensor(part, v_hi[:, :, 1, :], part, ALU.add))
                link(nc.vector.tensor_tensor(part, v_hi[:, :, 0, :], part, ALU.add))
                dst = rows[own, bass.ds(p * T + min(PLAN[2 * k][2], PLAN[2 * k + 1][2]) * P, 2 * P)]
                nc.vector.tensor_tensor(dst, dst, part.rearrange("p u n -> p (u n)"), ALU.mult).then_inc(o_done.sem, 1)

            def pair(i, s, more):
                p = i * 2 + s
                for u, h, b, r, n in PLAN:
                    if u + 1 < UNITS:
                        products(p, u + 1)
                    elif more:
                        products(p + 1, 0)
                    for x in range(n):
                        cnt, bank = min(4, b + 1 - 4 * x), (r + x) % 2
                        dve.wait_ge(*ahi_done.after(p * ROUNDS + r + x))
                        low(att[:, 4 * x:4 * x + cnt, 1, :],
                            ps[2][:, bank * HALF:bank * HALF + cnt * P].rearrange("p (k n) -> p k n", k=cnt),
                            att[:, 4 * x:4 * x + cnt, 0, :]).then_inc(alo_done.sem, 1)
                    if u % 2 == 0 and u > 0:
                        o_join(p, u // 2 - 1)
                    if more and u in (Q_AT, K_AT, V_AT + 1):
                        kind = (Q_AT, K_AT, V_AT + 1).index(u)
                        if kind == 1:
                            dve.wait_ge(*qlo_done.after(p + 1))
                        if kind == 2:
                            dve.wait_ge(*klo_done.after(2 * p + 3))
                        scaled(i * 6 + 3 * s + 3 + kind + N_QKV)
                    if more and u == Q_AT + 2:
                        q_low(p + 1, 1 - s)
                    if more and u == K_AT + 2:
                        k_double(p + 1, 1 - s)
                    if more and u == V_AT + 3:
                        v_low(p + 1, 1 - s)
                    if u == UNITS - 1:
                        o_join(p, KD - 1)

            scaled(N_QKV)
            q_low(0, 0)
            dve.wait_ge(*qlo_done.after(0))
            scaled(N_QKV + 1)
            k_double(0, 0)
            dve.wait_ge(*klo_done.after(1))
            scaled(N_QKV + 2)
            v_low(0, 0)
            products(0, 0)
            with dve.Fori(0, PAIRS // 2 - 1) as i:
                link.enter(i, 4 * KD)
                for s in range(2):
                    pair(i, s, True)
                link.leave(PAIRS // 2 - 1)
            pair(PAIRS // 2 - 1, 0, True)
            pair(PAIRS // 2 - 1, 1, False)

            dve.wait_ge(*olo_ready.after(PAIRS - 1))
            for dt in range(KD):
                dve.wait_ge(*w_used.after(N_OUT2 + dt))
                dve.wait_ge(x1_loaded[dt % 2], 16 * (dt // 2 + 1))
                nc.vector.tensor_tensor(rows[:, at(dt)], ps[dt % 2][:, :], fin_x[:, dt % 2, :], ALU.add).then_inc(x2_done.sem, 1)
                if dt:
                    add_square(dt, 2)
            invert(2)
            dve.wait_ge(*scale_ready.after(2))
            dve.wait_ge(*gain_done.after(KD - 1))
            for k in (0, 1, 2, 4, 5, 6):
                nc.vector.tensor_tensor(fin_out[:, k, :], rows[:, at(k)], scale[:, :], ALU.mult).then_inc(fin_dve.sem, 1)

        @block.tensor
        def _(pe):
            def sums(t):
                pe.wait_ge(*sq_added.after((KD - 1) * (t + 1) - 1))
                total = sq_buf[t][0]
                for k in range(KD):
                    ins = nc.tensor.matmul(ps[3][:, k:k + 1], total[:, at(k, P)], ones[:, :], start=True, stop=True)
                ins.then_inc(sums_done.sem, 1)

            def spread(t):
                pe.wait_ge(*rstd_ready.after(t))
                for k in range(KD):
                    ins = nc.tensor.matmul(ps[2][:, at(k, P)], rstd[:, k:k + 1].to_broadcast([P, P]), ident[:, :],
                                           start=True, stop=True)
                ins.then_inc(rstd_spread.sem, 1)

            def tile_product(dst, wh, wl, hi, lo, first, last):
                for s in range(2):
                    cols = at(s, HALF)
                    nc.tensor.matmul(dst[:, cols], wh, split[:, hi + s * HALF:hi + s * HALF + HALF], start=first, stop=False)
                    nc.tensor.matmul(dst[:, cols], wh, split[:, lo + s * HALF:lo + s * HALF + HALF], start=False, stop=False)
                for s in range(2):
                    ins = nc.tensor.matmul(dst[:, at(s, HALF)], wl, split[:, hi + s * HALF:hi + s * HALF + HALF], start=False, stop=last)
                return ins

            def chunk(m, c, dst):
                return tile_product(dst, w_hi[:, m, at(c, P)], w_lo[:, m, at(c, P)], c * T, (KD + c) * T, c == 0, c == KD - 1)

            def project(n, m, dst, ready=None):
                pe.wait_ge(*w_lo_ready.after(n))
                for c in range(KD):
                    if ready is not None:
                        pe.wait_ge(*ready(c))
                    ins = chunk(m, c, dst)
                ins.then_inc(w_used.sem, 1)

            pe.wait_ge(consts, 5)
            sums(0)
            spread(0)

            def gate_products(J, j):
                pe.wait_ge(*gw_lo_ready.after(J))
                pe.wait_ge(*ri_sig.after(J - 1))
                pe.wait_ge(*xblo_ready.after(J + 1 if j < GRP - 1 else J))
                slots = [s for s in range(3) if 0 <= j - 1 + s < GRP]
                for s in slots:
                    src = (j - 1 + s) % 3
                    for o in range(2):
                        w = slice(s * 256 + o * P, s * 256 + o * P + P)
                        ins = tile_product(ps[2 + o], gw_hi[:, w], gw_lo[:, w], (16 + src) * T, (19 + src) * T,
                                           s == slots[0], s == slots[-1])
                ins.then_inc(ri_done.sem, 1)

            pe.wait_ge(*scale_ready.after(0))
            with pe.Fori(0, 2) as g:
                for j in range(GRP):
                    J = g * GRP + j
                    pe.wait_ge(*taps_ready.after(J - 1))
                    project(J * 2, 0, ps[0], hlo_ready.after if j == 0 else None)
                    pe.wait_ge(*gated_done.after(J - 1))
                    project(J * 2 + 1, 1, ps[1])
                    if j > 0:
                        gate_products(J - 1, j - 1)
                    if j == GRP - 1:
                        gate_products(J, j)
            with pe.Fori(0, KD // 2) as i:
                for m in range(2):
                    for q in range(2):
                        n = i * 4 + 2 * m + q + N_IN
                        pe.wait_ge(*w_lo_ready.after(n))
                        if m == 0:
                            pe.wait_ge(*x1_done.after(i * 2 + q - 2))
                        for c5 in range(GRP):
                            c = m * GRP + c5
                            if q == 0:
                                pe.wait_ge(*(ylo_pool.after(c) if c < LT - 1 else ylo_dve.after(0)))
                            ins = tile_product(ps[q], w_hi[:, q, at(c5, P)], w_lo[:, q, at(c5, P)], *y_col(c), c == 0, c == LT - 1)
                        ins.then_inc(w_used.sem, 1)

            pe.wait_ge(*x1_done.after(KD - 2))
            project(N_GATE, 0, ps[0], lambda c: hlo_ready.after(KD + c))
            sums(1)
            pe.wait_ge(*x1_done.after(KD - 1))
            project(N_GATE + 1, 1, ps[1])
            spread(1)
            with pe.Fori(1, PAIRS // 2) as i:
                for m in range(2):
                    pe.wait_ge(*pg_done.after(i * 2 + m - 2))
                    project(i * 2 + m + N_GATE, m, ps[m])

            def turn_v(p):
                pe.wait_ge(*proj_done.after(p * 3 + 2))
                for k in range(KD):
                    ins = nc.tensor.transpose(ps[0][:, at(k, P)], proj[:, at(k, P)], ident[:, :])
                ins.then_inc(vturn_done.sem, 1)

            def fill(i, s, u):
                p = i * 2 + s + 1
                for x in range(sum(FILL[:u]), sum(FILL[:u + 1])):
                    kind, ch = divmod(x, KD)
                    c = 3 * s + 3 + kind + N_QKV
                    if ch == 0:
                        pe.wait_ge(*w_lo_ready.after(i * 6 + c))
                        pe.wait_ge(*(vlo_done.after(p - 1) if kind == 0 else proj_done.after(p * 3 + kind - 1)))
                    ins = chunk(c % 2, ch, ps[0])
                    if ch == KD - 1:
                        ins.then_inc(w_used.sem, 1)

            def scores(p, s, u):
                h, b = PLAN[u][1:3]
                lo = T - (b + 1) * P
                own, blk = slice(h * HD, h * HD + HD), at(b, P)
                if u == 0:
                    pe.wait_ge(*qlo_done.after(p))
                    pe.wait_ge(*klo_done.after(2 * p + 1))
                    pe.wait_ge(*kdup_done.after(p))
                for a, e in ((max(lo, HALF), T), (lo, HALF)):
                    if a >= e:
                        continue
                    keys = slice(a - lo, e - lo)
                    nc.tensor.matmul(ps[1][:, a:e], q_pair[:, s, h, blk], k_pair[:, s, h, keys], start=True, stop=False)
                    ins = nc.tensor.matmul(ps[1][:, a:e], q_pair[own, s, h, blk], k_low[own, s, keys], start=False, stop=e < T)
                    if e == T:
                        ins = nc.tensor.matmul(ps[1][:, T - P:T], ident_b[:, :], mask[:, :], start=False, stop=True)
                ins.then_inc(z_ready.sem, 1)

            def turn(p, u, h, b, r, n):
                pe.wait_ge(*att_done.after(p * UNITS + u))
                lo = T - (b + 1) * P
                for x in range(n):
                    bank = (r + x) % 2
                    pe.wait_ge(*alo_done.after(p * ROUNDS + r + x - 2))
                    for y in range(4 * x, min(4 * x + 4, b + 1)):
                        ins = nc.tensor.transpose(ps[2][:, bank * HALF + (y % 4) * P:bank * HALF + (y % 4) * P + P],
                                                  beta[:, u % 2, lo + y * P:lo + y * P + P], ident[:, :])
                    ins.then_inc(turn_done.sem, 1)

            def values(p, s, u, h, b, r, n):
                bank = (u // 2) % 2
                if u % 2 == 0:
                    pe.wait_ge(*o_done.after(p * KD + u // 2 - 2))
                if u == 0:
                    pe.wait_ge(*vlo_done.after(p))
                col = bank * HALF + (b % 2) * 2 * P
                for x in range(n):
                    pe.wait_ge(*alo_done.after(p * ROUNDS + r + x))
                    for y in range(4 * x, min(4 * x + 4, b + 1)):
                        ins = nc.tensor.matmul(ps[3][:, col:col + 2 * P], v_pair[:, s, y, h, :],
                                               att[:, y, :, :].rearrange("p x n -> p (x n)"), start=y == 0, stop=y == b)
                ins.then_inc(av_done.sem, 1)

            def pair(i, s, more):
                p = i * 2 + s
                for u, h, b, r, n in PLAN:
                    turn(p, u, h, b, r, n)
                    if u + 2 < UNITS or more:
                        pe.wait_ge(*sig_done.after(p * UNITS + u + 1))
                        if u + 2 < UNITS:
                            scores(p, s, u + 2)
                        else:
                            scores(p + 1, 1 - s, u + 2 - UNITS)
                    if more:
                        fill(i, s, u)
                    if more and u == V_AT + 2:
                        turn_v(p + 1)
                    if not more and 0 <= u - OUT_AT < PAIRS - 1:
                        if u == OUT_AT:
                            pe.wait_ge(*w_lo_ready.after(N_OUT2))
                            pe.wait_ge(*vlo_done.after(PAIRS - 1))
                        pe.wait_ge(*olo_ready.after(u - OUT_AT))
                        chunk(0, u - OUT_AT, ps[0])
                    values(p, s, u, h, b, r, n)

            pe.wait_ge(*pg_done.after(PAIRS - 2))
            project(N_QKV, 0, ps[0])
            pe.wait_ge(*proj_done.after(0))
            project(N_QKV + 1, 1, ps[0])
            pe.wait_ge(*proj_done.after(1))
            project(N_QKV + 2, 0, ps[0])
            pe.wait_ge(*pg_done.after(PAIRS - 1))
            scores(0, 0, 0)
            turn_v(0)
            pe.wait_ge(*sig_done.after(0))
            scores(0, 0, 1)
            with pe.Fori(0, PAIRS // 2 - 1) as i:
                for s in range(2):
                    pair(i, s, True)
            pair(PAIRS // 2 - 1, 0, True)
            pair(PAIRS // 2 - 1, 1, False)

            pe.wait_ge(*olo_ready.after(PAIRS - 1))
            chunk(0, KD - 1, ps[0]).then_inc(w_used.sem, 1)
            project(N_OUT2 + 1, 1, ps[1])
            with pe.Fori(1, KD // 2) as i:
                for q in range(2):
                    pe.wait_ge(*x2_done.after(i * 2 + q - 2))
                    project(i * 2 + q + N_OUT2, q, ps[q])
            sums(2)
            spread(2)


def kernel(**inputs):
    import numpy as np
    import concourse.bacc as bacc
    from concourse.bass_utils import run_bass_kernel_spmd

    a = {k: np.asarray(v) for k, v in inputs.items()}

    def cols(v):
        return v.reshape(-1, P).T

    heads, blk = a["lru_w_gates"].shape[1], a["lru_w_gates"].shape[2]
    bg = a["lru_b_gates"][0]
    params = np.concatenate(
        [cols(a["norm_g"][0]), cols(a["norm_g"][1])] + [cols(a["lru_conv_w"][0, t]) for t in range(4)]
        + [cols(a["lru_conv_b"][0]), cols(np.ascontiguousarray(bg[:, :blk]).reshape(-1)),
           cols(np.ascontiguousarray(bg[:, blk:]).reshape(-1)), cols(a["lru_lambda"][0]), cols(a["final_norm_g"])], axis=1)
    full = np.zeros((2, LRU, LRU), np.float32)
    for h in range(heads):
        s = slice(h * blk, h * blk + blk)
        full[0, s, s] = a["lru_w_gates"][0, h, :, :blk]
        full[1, s, s] = a["lru_w_gates"][0, h, :, blk:]
    w_gate = np.zeros((LT, P, 3, 2, P), np.float32)
    for t in range(LT):
        for s in range(3):
            if 0 <= t - 1 + s < LT:
                w_gate[t, :, s] = full[:, (t - 1 + s) * P:(t + s) * P, t * P:(t + 1) * P].transpose(1, 0, 2)
    w_gate = w_gate.reshape(LT, P, 3 * 256)

    def tiles(w, chunks):
        k, n = w.shape
        return w.reshape(k // (P * chunks), chunks, P, n // P, P).transpose(3, 0, 2, 1, 4).reshape(n // P, -1, P, chunks * P)

    wi = tiles(a["lru_w_in"][0], KD)[:, 0]
    wi = np.stack([wi[:LT], wi[LT:]], axis=1).reshape(N_IN, P, D)
    wo = tiles(a["lru_w_out"][0], GRP).reshape(KD // 2, 2, 2, P, GRP * P).transpose(0, 2, 1, 3, 4).reshape(2 * KD, P, GRP * P)
    wo = np.concatenate([wo, np.zeros((2 * KD, P, D - GRP * P), np.float32)], axis=2)
    sbw = tiles(a["sb_w_in"][0], KD)[:, 0].reshape(4, KD, P, D).transpose(1, 0, 2, 3).reshape(4 * KD, P, D)
    sbo = tiles(a["sb_w_out"][0], KD)[:, 0]
    weights = np.concatenate([wi, wo, sbw[3::4], sbw.reshape(KD, 4, P, D)[:, :3].reshape(3 * KD, P, D), sbo], axis=0)
    host = {"xT": np.ascontiguousarray(a["x"][0].T).reshape(KD, P, T), "params": params, "weights": weights, "w_gate": w_gate}

    nc = bacc.Bacc("TRN2", target_bir_lowering=False, num_devices=1)
    arrays, args = {}, []
    for name, v in host.items():
        v = np.ascontiguousarray(v)
        arrays[f"in_{name}"] = v
        args.append(nc.dram_tensor(f"in_{name}", v.shape, mybir.dt.from_np(v.dtype), kind="ExternalInput").ap())
    out = nc.dram_tensor("out_dram", (KD, P, T), mybir.dt.float32, kind="ExternalOutput").ap()
    kept = nc.dram_tensor("kept_x1", (KD, P, T), mybir.dt.float32, kind="Internal").ap()
    build(nc, *args, kept, out)
    r = run_bass_kernel_spmd(nc, [arrays], core_ids=[0])
    return r.results[0]["out_dram"].reshape(D, T).T.reshape(1, T, D)
```

```python
import concourse.bass as bass
from concourse import mybir
from contextlib import ExitStack

P = 128
T = 1024
D = 1024
KD = D // P
HALF = 512
LRU = 1280
LT = LRU // P
GRP = 5
EPS = 1e-6
N_IN = 2 * LT
N_GATE = N_IN + 2 * KD
PAIRS = 8
HD = 64
N_QKV = N_GATE + PAIRS
N_OUT2 = N_QKV + 3 * PAIRS
N_ALL = N_OUT2 + KD
UNITS = 16
V_ROUNDS = 2
ROUNDS = 24 + V_ROUNDS
SCALE = HD ** -0.5
MASKED = -1e30
PAR_G, PAR_CW, PAR_CB, PAR_BR, PAR_BI, PAR_LAM, PAR_FG = 0, 16, 56, 66, 76, 86, 96
PAR = 104


def build(nc, xT, params, weights, w_gate, kept, out):
    F32, F32R, BF16 = mybir.dt.float32, mybir.dt.float32r, mybir.dt.bfloat16
    ALU, ACT = mybir.AluOpType, mybir.ActivationFunctionType

    ctx = ExitStack()
    with ctx:
        def sb(name, shape, dt=F32):
            return ctx.enter_context(nc.sbuf_tensor(name, shape, dt))

        def sem(name):
            return ctx.enter_context(nc.semaphore(name))

        class Count:
            def __init__(self, name, credit=0):
                self.sem, self.credit = sem(name), credit

            def after(self, t):
                return self.sem, t + 1 + self.credit

        split = sb("split", [P, 22 * T], F32R)
        h_hi, h_lo = split[:, 0:KD * T], split[:, KD * T:2 * KD * T]
        xb_hi, xb_lo = split[:, 16 * T:19 * T], split[:, 19 * T:22 * T]
        rows = sb("rows", [P, LT * T])
        w_stage = sb("w_stage", [P, D])
        w_hi = sb("w_hi", [P, 2, D], F32R)
        w_lo = sb("w_lo", [P, 2, D], F32R)
        scale = sb("scale", [P, T])
        par = sb("par", [P, PAR])
        tiny = sb("tiny", [P, 7, LT])
        ones = sb("ones", [P, 1])
        eps = sb("eps", [P, 1])
        zero = sb("zero", [P, 1])
        ident = sb("ident", [P, P])
        rstd = sb("rstd", [P, KD])
        ident_b = sb("ident_b", [P, P], BF16)
        mask = sb("mask", [P, P], BF16)
        with ExitStack() as turn:
            def tb(name, shape, dt=F32):
                return turn.enter_context(nc.sbuf_tensor(name, shape, dt))
            gw_stage = tb("gw_stage", [P, 3 * 256])
            gw_hi = tb("gw_hi", [P, 3 * 256], F32R)
            gw_lo = tb("gw_lo", [P, 3 * 256], F32R)
            taps = tb("taps", [P, T + 4])
            conv = tb("conv", [P, 3, T])
            gated = tb("gated", [P, 3, T])
            work = tb("work", [P, 4, T])
        with ExitStack() as turn:
            q_pair = tb("q_pair", [P, 2, 2, T], F32R)
            v_pair = tb("v_pair", [P, 2, KD, 2, P], F32R)
            att = tb("att", [P, KD, 2, P], F32R)
            fail = tb("fail", [P, 2, T + 1])
            proj = tb("proj", [P, T])
            o_part = tb("o_part", [P, 2, P])
        with ExitStack() as turn:
            fin_sum = tb("fin_sum", [P, T])
            fin_sq = tb("fin_sq", [P, 2, T])
            fin_x = tb("fin_x", [P, 2, T])
            fin_out = tb("fin_out", [P, KD, T])
        k_pair = split[:, 16 * T:20 * T].rearrange("p (s h n) -> p s h n", s=2, h=2)
        k_low = split[:, 20 * T:22 * T].rearrange("p (s n) -> p s n", s=2)
        beta = rows[:, 8 * T:10 * T].rearrange("p (s n) -> p s n", s=2)
        sq_buf = {0: (gated[:, 2, :], gated), 1: (gated[:, 2, :], gated), 2: (fin_sum[:, :], fin_sq)}
        SPARE = (LT - 3) % 3

        def lru_work(J):
            if J < LT - 1:
                return [work[:, i, :] for i in range(4)]
            return [taps[:, 0:T], conv[:, SPARE, :], gated[:, SPARE, :], scale[:, :]]
        ps = [ctx.enter_context(nc.psum_tensor(f"ps{i}", [P, T], F32)) for i in range(4)]

        x_loaded = [sem(f"x_loaded{i}") for i in range(KD)]
        par_loaded, w_loaded, gw_loaded, x1_kept = sem("par_loaded"), sem("w_loaded"), sem("gw_loaded"), sem("x1_kept")
        xs_loaded = [sem("xs_loaded0"), sem("xs_loaded1")]
        x1_loaded = [sem("x1_loaded0"), sem("x1_loaded1")]
        stored = sem("stored")
        act_step, dve_step, pool_step, decay_ready, consts = (
            sem("act_step"), sem("dve_step"), sem("pool_step"), sem("decay_ready"), sem("consts"))
        w_hi_ready, w_lo_ready, w_used = Count("w_hi_ready"), Count("w_lo_ready"), Count("w_used", 2)
        gw_hi_ready, gw_lo_ready = Count("gw_hi_ready"), Count("gw_lo_ready", 1)
        sq_ready, sq_added = Count("sq_ready"), Count("sq_added")
        sums_done, root_done, rstd_ready, rstd_spread, scale_ready = (
            Count("sums_done"), Count("root_done"), Count("rstd_ready"), Count("rstd_spread"), Count("scale_ready"))
        hhi_ready, hlo_ready = Count("hhi_ready"), Count("hlo_ready")
        taps_ready, conv_done = Count("taps_ready", 1), Count("conv_done", 1)
        xbhi_ready, xblo_ready = Count("xbhi_ready"), Count("xblo_ready", 2)
        gated_done, gsig_done, gsilu_done = Count("gated_done", 1), Count("gsig_done"), Count("gsilu_done")
        ri_done, ri_sig, root_ready, lru_done = Count("ri_done", 2), Count("ri_sig", 1), Count("root_ready"), Count("lru_done", 2)
        yhi_act, ylo_pool, ylo_dve = Count("yhi_act"), Count("ylo_pool"), Count("ylo_dve")
        x1_done = Count("x1_done", 2)
        pg_done, bsig_done, silu_done = Count("pg_done", 2), Count("bsig_done"), Count("silu_done", 2)
        proj_done = Count("proj_done")
        qhi_done, qlo_done = Count("qhi_done"), Count("qlo_done")
        khi_done, klo_done, kdup_done = Count("khi_done"), Count("klo_done"), Count("kdup_done")
        z_ready, sig_done, scan_done, att_done = Count("z_ready"), Count("sig_done"), Count("scan_done"), Count("att_done")
        turn_done, ahi_done, alo_done = Count("turn_done"), Count("ahi_done"), Count("alo_done", 2)
        av_done, opart_done, o_done = Count("av_done", 1), Count("opart_done"), Count("o_done", 2)
        ohi_ready, olo_ready = Count("ohi_ready"), Count("olo_ready")
        half_used, half_x2, half_sq, half_gain = Count("half_used"), Count("half_x2"), Count("half_sq"), Count("half_gain")
        x2_done, gain_done, fin_dve, fin_pool = Count("x2_done", 2), Count("gain_done"), Count("fin_dve"), Count("fin_pool")
        credited = [w_used, gw_lo_ready, taps_ready, conv_done, xblo_ready, gated_done, ri_done, ri_sig, lru_done,
                    x1_done, pg_done, silu_done, alo_done, av_done, o_done, x2_done]

        class Chain:
            def __init__(self, eng, s):
                self.eng, self.s, self.base, self.k = eng, s, 0, 0

            def __call__(self, ins):
                self.k += 1
                ins.then_inc(self.s, 1)
                self.eng.wait_ge(self.s, self.base + self.k)

            def enter(self, i, per):
                self.start, self.per = self.base + self.k, per
                self.base, self.k = self.start + i * per, 0

            def leave(self, trips):
                assert self.k == self.per, (self.k, self.per)
                self.base, self.k = self.start + trips * self.per, 0

        def at(t, n=T):
            return slice(t * n, t * n + n)

        def dram_tile(src, t):
            return src[bass.ds(t, 1)].rearrange("a p n -> p (a n)")

        def y_col(c):
            return (c * T, (KD + c) * T) if c < KD else ((8 + c) * T, (10 + c) * T)

        Y_POOL = range(GRP, LT - 1)

        def y_split(c):
            return ylo_pool.after(c - GRP) if c in Y_POOL else ylo_dve.after(c if c < GRP else GRP)

        PLAN, r = [], 0
        for u in range(UNITS):
            h, b = divmod(u, KD)
            b = KD - 1 - b if h else b
            PLAN.append((u, h, b, r, b // 4 + 1))
            r += b // 4 + 1 + (V_ROUNDS if u == UNITS - 2 else 0)
        assert r == ROUNDS
        PLACE = [3, 4, 0, 4, 0, 0, 0, 0, 0, 0, 0, 0, 0, 4, 0, 2]
        EARLY = (14, 15, 0)
        for u in EARLY:
            mine, last = (set(range(PLACE[x], PLACE[x] + PLAN[x][2] + 1)) for x in (u, (u - 1) % UNITS))
            assert not mine & last and max(mine) < KD
        FILL = [1, 1, 1, 1, 2, 2, 2, 2, 2, 2, 2, 2, 1, 1, 1, 1]
        assert sum(FILL) == 3 * KD
        AHEAD = 12
        FILLED = sum(FILL[AHEAD:])
        Q_AT, K_AT, V_AT = 3, 7, 11
        V_TURN_AT = UNITS - 2
        W_HI_AT = (Q_AT + 1, K_AT + 1, V_AT + 1)
        W_LO_AT = (Q_AT + 1, K_AT + 1, V_AT + 2), (Q_AT + 2, K_AT + 2, V_AT + 3)
        SPLIT_AT, OUT_AT = (1, 1, 2, 2, 3, 3, 4), (2, 3, 5, 7, 9, 11, 12)

        def left(u):
            return T - (PLAN[u % UNITS][2] + 1) * P

        def round_of(p, e, last=False):
            return p * ROUNDS + V_ROUNDS + PLAN[e % UNITS][3] + e // UNITS * ROUNDS - (V_ROUNDS if last and e == UNITS - 1 else 0)

        def v_round(p):
            return (p - 1) * ROUNDS + V_ROUNDS + PLAN[UNITS - 2][3] + PLAN[UNITS - 2][4] if not isinstance(p, int) or p else 0

        def v_bank(p, x):
            return (PLAN[UNITS - 1][3] + x) % 2 if not isinstance(p, int) or p else x

        block = ctx.enter_context(nc.Block())

        @block.sync
        def _(sp):
            def load_weights(n, width=D):
                sp.wait_ge(*w_lo_ready.after(n - 1))
                sp.dma_start(w_stage[:, 0:width], dram_tile(weights, n)[:, 0:width]).then_inc(w_loaded, 16)

            sp.dma_start(par[:, :], params).then_inc(par_loaded, 16)
            sp.dma_start(w_stage[:, :], weights[0]).then_inc(w_loaded, 16)
            for k in range(KD):
                sp.dma_start(rows[:, at(k)], xT[k]).then_inc(x_loaded[k], 16)
            load_weights(1)
            with sp.Fori(0, 2) as g:
                for j in range(GRP):
                    J = g * GRP + j
                    sp.wait_ge(*gw_lo_ready.after(J - 1))
                    sp.dma_start(gw_stage[:, :], dram_tile(w_gate, J)).then_inc(gw_loaded, 16)
                    for m in range(2):
                        load_weights(J * 2 + m + 2)
            def residual_load(dt, q):
                sp.wait_ge(*x1_done.after(dt - 2))
                sp.dma_start(work[:, q, :], dram_tile(xT, dt)).then_inc(xs_loaded[q], 16)

            for n in range(N_IN + 2, N_IN + 4):
                load_weights(n, GRP * P)
            sp.wait_ge(*lru_done.after(LT - 1))
            with sp.Fori(0, KD // 2 - 1) as i:
                for q in range(2):
                    dt = i * 2 + q
                    residual_load(dt, q)
                    for m in range(2):
                        load_weights(dt * 2 + m + N_IN + 4, GRP * P)
            for q in range(2):
                residual_load(KD - 2 + q, q)
                load_weights(N_GATE + q)
            with sp.Fori(0, KD) as k:
                sp.wait_ge(*x1_done.after(k))
                sp.dma_start(dram_tile(kept, k), rows[:, bass.ts(k, T)]).then_inc(x1_kept, 16)
            with sp.Fori(N_GATE + 2, N_OUT2 + 2) as n:
                load_weights(n)
            sp.wait_ge(x1_kept, 16 * KD)
            sp.wait_ge(*olo_ready.after(PAIRS - 1))

            def last_loads(dt, q, more):
                sp.wait_ge(*x2_done.after(dt - 2))
                sp.dma_start(fin_x[:, q, :], dram_tile(kept, dt)).then_inc(x1_loaded[q], 16)
                if more:
                    load_weights(dt + N_OUT2 + 2)
            with sp.Fori(0, KD // 2 - 1) as i:
                for q in range(2):
                    last_loads(i * 2 + q, q, True)
            for q in range(2):
                last_loads(KD - 2 + q, q, False)
            for half in range(2):
                for k in (0, 1, 3, 2):
                    sp.wait_ge(*(fin_pool.after(half) if k == 3 else fin_dve.after(3 * half + k)))
                    sp.dma_start(out[2 * k:2 * k + 2].rearrange("k p n -> p k n")[:, :, at(half, HALF)],
                                 fin_out[:, 2 * k:2 * k + 2, at(half, HALF)]).then_inc(stored, 16)
            sp.wait_ge(stored, 16 * KD)

        @block.gpsimd
        def _(pool):
            link = Chain(pool, pool_step)
            for c in credited:
                pool.sem_inc(c.sem, c.credit)
            nc.gpsimd.memset(ones[:, :], 1.0).then_inc(consts, 1)
            nc.gpsimd.memset(eps[:, :], EPS).then_inc(consts, 1)
            nc.gpsimd.memset(zero[:, :], 0.0).then_inc(consts, 1)
            nc.gpsimd.memset(taps[:, 0:4], 0.0).then_inc(consts, 1)
            link(nc.gpsimd.memset(ident[:, :], 0.0))
            nc.gpsimd.affine_select(out=ident[:, :], in_=ident[:, :], compare_op=ALU.not_equal, fill=1.0,
                                    base=0, pattern=[[-1, P]], channel_multiplier=1).then_inc(consts, 1)
            pool.wait_ge(consts, 5)
            nc.gpsimd.tensor_copy(ident_b[:, :], ident[:, :]).then_inc(consts, 1)
            link(nc.gpsimd.memset(mask[:, :], 0.0))
            nc.gpsimd.affine_select(out=mask[:, :], in_=mask[:, :], compare_op=ALU.is_ge, fill=MASKED,
                                    base=-1, pattern=[[-1, P]], channel_multiplier=1).then_inc(consts, 1)

            def low(dst, src, hi):
                return nc.gpsimd.tensor_tensor(dst, src, hi.bitcast(F32), ALU.subtract)

            def weight_lo(n, m, width=D):
                pool.wait_ge(*w_hi_ready.after(n))
                low(w_lo[:, m, 0:width], w_stage[:, 0:width], w_hi[:, m, 0:width]).then_inc(w_lo_ready.sem, 1)

            weight_lo(0, 0)
            total, ring = sq_buf[0]
            for k in range(1, KD):
                pool.wait_ge(*sq_ready.after(k))
                if k > 1:
                    pool.wait_ge(*sq_added.after(k - 2))
                nc.gpsimd.tensor_tensor(total, total, ring[:, k % 2, :], ALU.add).then_inc(sq_added.sem, 1)
            for J in range(LT):
                weight_lo(J * 2 + 2, 0)
                pool.wait_ge(*xbhi_ready.after(J))
                low(xb_lo[:, at(J % 3)], conv[:, J % 3, :], xb_hi[:, at(J % 3)]).then_inc(xblo_ready.sem, 1)
                weight_lo(J * 2 + 3, 1)
                pool.wait_ge(*gw_hi_ready.after(J))
                low(gw_lo[:, :], gw_stage[:, :], gw_hi[:, :]).then_inc(gw_lo_ready.sem, 1)
                pool.wait_ge(*gsig_done.after(J))
                nc.gpsimd.tensor_tensor(gated[:, J % 3, :], gated[:, J % 3, :], rows[:, at(J)], ALU.mult).then_inc(gsilu_done.sem, 1)
            for c in Y_POOL:
                hi, lo = y_col(c)
                pool.wait_ge(*yhi_act.after(c))
                low(split[:, lo:lo + T], rows[:, at(c)], split[:, hi:hi + T]).then_inc(ylo_pool.sem, 1)
                if c == GRP + 1:
                    weight_lo(N_IN + 2, 0, GRP * P)
            weight_lo(N_IN + 3, 1, GRP * P)
            with pool.Fori(N_IN // 2 + 2, N_GATE // 2) as i:
                for m in range(2):
                    weight_lo(i * 2 + m, m, GRP * P)
            for m in range(2):
                weight_lo(N_GATE + m, m)

            def silu(p, m):
                pool.wait_ge(*bsig_done.after(p))
                nc.gpsimd.tensor_tensor(rows[:, at(p) if isinstance(p, int) else bass.ts(p, T)],
                                        rows[:, at(p) if isinstance(p, int) else bass.ts(p, T)], beta[:, m, :],
                                        ALU.mult).then_inc(silu_done.sem, 1)
            weight_lo(N_GATE + 2, 0)
            weight_lo(N_GATE + 3, 1)
            silu(0, 0)
            silu(1, 1)
            with pool.Fori(1, PAIRS // 2) as i:
                for m in range(2):
                    silu(i * 2 + m, m)
                    weight_lo(i * 2 + m + N_GATE + 2, m)

            def k_lower(p, s, h):
                pool.wait_ge(*khi_done.after(p))
                own = slice(h * HD, h * HD + HD)
                low(k_low[own, s, :], proj[own, :], k_pair[own, s, h, :]).then_inc(klo_done.sem, 1)
                pool.wait_ge(*klo_done.after(2 * p + h))

            def weight_lo_half(n, m, half):
                if half == 0:
                    pool.wait_ge(*w_hi_ready.after(n))
                ins = low(w_lo[:, m, at(half, HALF)], w_stage[:, at(half, HALF)], w_hi[:, m, at(half, HALF)])
                if half == 1:
                    ins.then_inc(w_lo_ready.sem, 1)

            def attend(p, u):
                lo = left(u)
                pool.wait_ge(*scan_done.after(p * UNITS + u))
                nc.gpsimd.tensor_tensor(beta[:, u % 2, lo:T], beta[:, u % 2, lo:T], fail[:, u % 2, lo + 1:T + 1],
                                        ALU.mult).then_inc(att_done.sem, 1)

            def pair(i, s, more):
                p = i * 2 + s
                for e in range(1, UNITS + 1):
                    if e + 1 < UNITS:
                        attend(p, e + 1)
                    elif more:
                        attend(p + 1, e + 1 - UNITS)
                    if more and e in (K_AT + 3, K_AT + 4):
                        pool.wait_ge(*att_done.after(p * UNITS + e + 1))
                        k_lower(p + 1, 1 - s, e - K_AT - 3)
                    for half in range(2):
                        if more and e in W_LO_AT[half]:
                            c = 3 * s + W_LO_AT[half].index(e) + N_QKV + 5
                            weight_lo_half(i * 6 + c, c % 2, half)
            weight_lo(N_QKV + 2, 0)
            pool.wait_ge(*w_lo_ready.after(N_QKV + 2))
            k_lower(0, 0, 0)
            k_lower(0, 0, 1)
            weight_lo(N_QKV + 3, 1)
            attend(0, 0)
            attend(0, 1)
            weight_lo(N_QKV + 4, 0)
            with pool.Fori(0, PAIRS // 2 - 1) as i:
                for s in range(2):
                    pair(i, s, True)
            pair(PAIRS // 2 - 1, 0, True)
            pair(PAIRS // 2 - 1, 1, False)
            with pool.Fori(0, KD // 2 - 1) as i:
                for m in range(2):
                    weight_lo(i * 2 + m + N_OUT2 + 2, m)
            for half in range(2):
                cols = at(half, HALF)
                pool.wait_ge(*scale_ready.after(2 + half))
                pool.wait_ge(*half_gain.after(half))
                x = rows[:, (KD - 2) * T:KD * T].rearrange("p (k n) -> p k n", k=2)[:, :, cols]
                rms = scale[:, cols].rearrange("p (a n) -> p a n", a=1).to_broadcast([P, 2, HALF])
                nc.gpsimd.tensor_tensor(fin_out[:, KD - 2:KD, cols], x, rms, ALU.mult).then_inc(fin_pool.sem, 1)

        @block.scalar
        def _(act):
            link = Chain(act, act_step)

            def weight_hi(n, m, width=D):
                act.wait_ge(w_loaded, (n + 1) * 16)
                act.wait_ge(*w_used.after(n - 2))
                nc.scalar.copy(w_hi[:, m, 0:width], w_stage[:, 0:width]).then_inc(w_hi_ready.sem, 1)

            def square(k, t):
                total, ring = sq_buf[t]
                if k >= 3:
                    act.wait_ge(*sq_added.after((KD - 1) * t + k - 3))
                dst = total if k == 0 else ring[:, k % 2, :]
                nc.scalar.activation(dst, rows[:, at(k)], ACT.Square).then_inc(sq_ready.sem, 1)

            def h_high(k, gain):
                nc.scalar.activation(h_hi[:, at(k)], rows[:, at(k)], ACT.Copy, scale=par[:, gain + k:gain + k + 1]).then_inc(hhi_ready.sem, 1)

            def root(t):
                act.wait_ge(*sums_done.after(t))
                nc.scalar.activation(rstd[:, :], ps[3][:, 0:KD], ACT.Sqrt, bias=eps[:, :], scale=1.0 / D).then_inc(root_done.sem, 1)

            def keep_scale(t):
                act.wait_ge(*rstd_spread.after(t))
                nc.scalar.copy(scale[:, :], ps[2][:, :]).then_inc(scale_ready.sem, 1)

            act.wait_ge(par_loaded, 16)
            link(nc.scalar.activation(tiny[:, 0, :], par[:, PAR_LAM:PAR_LAM + LT], ACT.Abs))
            link(nc.scalar.activation(tiny[:, 0, :], tiny[:, 0, :], ACT.Exp, scale=-1.0))
            weight_hi(0, 0)
            for k in range(KD):
                act.wait_ge(x_loaded[k], 16)
                h_high(k, PAR_G)
                square(k, 0)
            weight_hi(1, 1)
            act.wait_ge(consts, 5)
            root(0)
            weight_hi(2, 0)
            keep_scale(0)

            def y_high(c):
                act.wait_ge(*w_used.after(N_IN - 1))
                act.wait_ge(*lru_done.after(c))
                hi, lo = y_col(c)
                nc.scalar.copy(split[:, hi:hi + T], rows[:, at(c)]).then_inc(yhi_act.sem, 1)

            def gate_sigmoids(J):
                r, gi = lru_work(J)[:2]
                act.wait_ge(*ri_done.after(J))
                act.wait_ge(*lru_done.after(J - 1 if J < LT - 1 else J - 2))
                nc.scalar.activation(gi, ps[3][:, :], ACT.Sigmoid, bias=par[:, PAR_BI + J:PAR_BI + J + 1])
                nc.scalar.activation(r, ps[2][:, :], ACT.Sigmoid, bias=par[:, PAR_BR + J:PAR_BR + J + 1]).then_inc(ri_sig.sem, 1)

            def gates(J):
                r, gi, rt, a = lru_work(J)
                act.wait_ge(*ri_sig.after(J))
                nc.scalar.activation(a, r, ACT.Exp, scale=tiny[:, 6, J:J + 1])
                link(nc.scalar.activation(r, r, ACT.Tanh, scale=tiny[:, 5, J:J + 1]))
                nc.scalar.activation(rt, r, ACT.Sqrt).then_inc(root_ready.sem, 1)

            act.wait_ge(decay_ready, 1)
            for J in range(LT):
                if J:
                    weight_hi(J * 2 + 2, 0)
                act.wait_ge(*conv_done.after(J))
                if J >= 3:
                    act.wait_ge(*ri_done.after(J - 2))
                nc.scalar.copy(xb_hi[:, at(J % 3)], conv[:, J % 3, :]).then_inc(xbhi_ready.sem, 1)
                weight_hi(J * 2 + 3, 1)
                act.wait_ge(*gated_done.after(J))
                nc.scalar.activation(rows[:, at(J)], gated[:, J % 3, :], ACT.Sigmoid).then_inc(gsig_done.sem, 1)
                if J == LT - 1:
                    for c in range(2):
                        y_high(c)
                act.wait_ge(gw_loaded, (J + 1) * 16)
                act.wait_ge(*ri_done.after(J - 1))
                nc.scalar.copy(gw_hi[:, :], gw_stage[:, :]).then_inc(gw_hi_ready.sem, 1)
                if J > 0:
                    gate_sigmoids(J - 1)
                    if J == LT - 1:
                        for c in range(2, GRP):
                            y_high(c)
                    gates(J - 1)
            gate_sigmoids(LT - 1)
            y_high(GRP)
            y_high(GRP + 1)
            weight_hi(N_IN + 2, 0, GRP * P)
            y_high(GRP + 2)
            gates(LT - 1)
            y_high(LT - 2)
            weight_hi(N_IN + 3, 1, GRP * P)
            y_high(LT - 1)
            for i in range(KD // 2):
                n = N_IN + 4 * i + 2
                last = i == KD // 2 - 1
                if i:
                    for q in range(2):
                        weight_hi(n + q, q, GRP * P)
                if last:
                    act.wait_ge(*w_used.after(n - 1))
                    for k in range(GRP):
                        h_high(k, PAR_G + KD)
                for q in range(2):
                    weight_hi(n + 2 + q, q, D if last else GRP * P)
                    act.wait_ge(*x1_done.after(2 * i + q))
                    square(2 * i + q, 1)

            act.wait_ge(*w_used.after(N_GATE - 1))
            for k in range(GRP, KD):
                h_high(k, PAR_G + KD)
            weight_hi(N_GATE + 2, 0)
            root(1)
            keep_scale(1)
            weight_hi(N_GATE + 3, 1)

            def gate_sigmoid(p, m):
                act.wait_ge(*pg_done.after(p))
                act.wait_ge(*silu_done.after(p - 2))
                nc.scalar.activation(beta[:, m, :], rows[:, at(p) if isinstance(p, int) else bass.ts(p, T)], ACT.Sigmoid).then_inc(bsig_done.sem, 1)
            gate_sigmoid(0, 0)
            gate_sigmoid(1, 1)
            with act.Fori(1, PAIRS // 2) as i:
                for m in range(2):
                    gate_sigmoid(i * 2 + m, m)
                    weight_hi(i * 2 + m + N_GATE + 2, m)

            def q_high(p, s):
                act.wait_ge(*proj_done.after(p * 3))
                for h in range(2):
                    own = slice(h * HD, h * HD + HD)
                    ins = nc.scalar.copy(q_pair[own, s, h, :], proj[own, :])
                ins.then_inc(qhi_done.sem, 1)

            def k_high(p, s):
                act.wait_ge(*proj_done.after(p * 3 + 1))
                for h in range(2):
                    own = slice(h * HD, h * HD + HD)
                    ins = nc.scalar.copy(k_pair[own, s, h, :], proj[own, :])
                ins.then_inc(khi_done.sem, 1)

            def v_high(p, s):
                for x in range(V_ROUNDS):
                    act.wait_ge(*turn_done.after(v_round(p) + x))
                    nc.scalar.copy(v_pair[:, s, 4 * x:4 * x + 4, :, 0:HD], ps[2][:, at(v_bank(p, x), HALF)].rearrange(
                        "p (k h d) -> p k h d", k=4, h=2)).then_inc(ahi_done.sem, 1)

            def sigmoids(p, u, free=True):
                lo = left(u)
                U = p * UNITS + u
                act.wait_ge(*z_ready.after(U))
                if free:
                    prev = PLAN[(u - 2) % UNITS]
                    act.wait_ge(*att_done.after(U - 2))
                    act.wait_ge(*turn_done.after(p * ROUNDS + V_ROUNDS + (prev[3] + prev[4] - 1 - (ROUNDS if u < 2 else 0))))
                nc.scalar.activation(fail[:, u % 2, lo:T], ps[1][:, lo:T], ACT.Sigmoid, scale=-SCALE)
                nc.scalar.activation(beta[:, u % 2, lo:T], ps[1][:, lo:T], ACT.Sigmoid, scale=SCALE).then_inc(sig_done.sem, 1)

            def o_second(p, k):
                h, bank = k // 4, k % 2
                act.wait_ge(*av_done.after(p * UNITS + 2 * k + 1))
                act.wait_ge(*o_done.after(p * KD + k - 1))
                nc.scalar.copy(o_part[h * HD:h * HD + HD, :, :],
                               ps[3][HD:P, at(bank, HALF)].rearrange("p (u x n) -> p u x n", u=2, x=2)[:, :, 0, :]).then_inc(opart_done.sem, 1)

            def o_high(p):
                act.wait_ge(*o_done.after(p * KD + KD - 1))
                nc.scalar.copy(h_hi[:, at(p)], rows[:, at(p)]).then_inc(ohi_ready.sem, 1)

            def att_high(p, e, first=False, last=False):
                h, b, r, n = PLAN[e % UNITS][1:]
                if not first:
                    act.wait_ge(*av_done.after(p * UNITS + e - (2 if e % UNITS in EARLY else 1)))
                for x in range(n):
                    cnt, bank, place = min(4, b + 1 - 4 * x), (r + x) % 2, PLACE[e % UNITS] + 4 * x
                    act.wait_ge(*turn_done.after(round_of(p, e, last) + x))
                    nc.scalar.copy(att[:, place:place + cnt, 0, :],
                                   ps[2][:, bank * HALF:bank * HALF + cnt * P].rearrange("p (k n) -> p k n", k=cnt)).then_inc(ahi_done.sem, 1)

            def pair(i, s, more):
                p = i * 2 + s
                for e in range(1, UNITS + 1):
                    if e < UNITS or more:
                        att_high(p, e, last=not more)
                    if e + 2 < UNITS:
                        sigmoids(p, e + 2)
                    elif more:
                        sigmoids(p + 1, e + 2 - UNITS)
                    if e % 2 == 0:
                        o_second(p, e // 2 - 1)
                    if more and e == Q_AT + 1:
                        q_high(p + 1, 1 - s)
                    if more and e == K_AT + 1:
                        k_high(p + 1, 1 - s)
                    if more and e in W_HI_AT:
                        c = 3 * s + W_HI_AT.index(e) + N_QKV + 5
                        weight_hi(i * 6 + c, c % 2)
                    if more and e == V_TURN_AT:
                        v_high(p + 1, 1 - s)
                    if not more and e == 1:
                        act.wait_ge(*w_used.after(N_OUT2 - 1))
                    for c in range(PAIRS - 1):
                        if not more and e == SPLIT_AT[c]:
                            o_high(c)

            q_high(0, 0)
            weight_hi(N_QKV + 2, 0)
            k_high(0, 0)
            weight_hi(N_QKV + 3, 1)
            sigmoids(0, 0, False)
            sigmoids(0, 1, False)
            v_high(0, 0)
            att_high(0, 0, True)
            sigmoids(0, 2)
            weight_hi(N_QKV + 4, 0)
            with act.Fori(0, PAIRS // 2 - 1) as i:
                for s in range(2):
                    pair(i, s, True)
            pair(PAIRS // 2 - 1, 0, True)
            pair(PAIRS // 2 - 1, 1, False)
            o_high(PAIRS - 1)

            for dt in range(KD - 1):
                if dt < KD - 2:
                    weight_hi(N_OUT2 + dt + 2, dt % 2)
                act.wait_ge(*x2_done.after(dt))
                square(dt, 2)
                nc.scalar.activation(rows[:, at(dt)], rows[:, at(dt)], ACT.Copy, scale=par[:, PAR_FG + dt:PAR_FG + dt + 1]).then_inc(gain_done.sem, 1)
            act.wait_ge(*sq_added.after(3 * KD - 6))
            for half in range(2):
                x2 = rows[:, (KD - 1) * T + half * HALF:(KD - 1) * T + half * HALF + HALF]
                act.wait_ge(*half_x2.after(half))
                nc.scalar.activation(fin_sq[:, 1, at(half, HALF)], x2, ACT.Square).then_inc(half_sq.sem, 1)
                nc.scalar.activation(x2, x2, ACT.Copy, scale=par[:, PAR_FG + KD - 1:PAR_FG + KD]).then_inc(half_gain.sem, 1)
                act.wait_ge(*sums_done.after(2 + half))
                tok = slice(half * KD // 2, (half + 1) * KD // 2)
                nc.scalar.activation(rstd[:, tok], ps[3][:, tok], ACT.Sqrt, bias=eps[:, :], scale=1.0 / D).then_inc(root_done.sem, 1)
                act.wait_ge(*rstd_spread.after(2 + half))
                nc.scalar.copy(scale[:, at(half, HALF)], ps[2][:, at(half, HALF)]).then_inc(scale_ready.sem, 1)

        @block.vector
        def _(dve):
            link = Chain(dve, dve_step)
            def low(dst, src, hi):
                return nc.vector.tensor_tensor(dst, src, hi.bitcast(F32), ALU.subtract)

            def add_square(k, t):
                dve.wait_ge(*sq_ready.after(KD * t + k))
                if k > 1:
                    dve.wait_ge(*sq_added.after((KD - 1) * t + k - 2))
                total, ring = sq_buf[t]
                nc.vector.tensor_tensor(total, total, ring[:, k % 2, :], ALU.add).then_inc(sq_added.sem, 1)

            def h_lower(k, gain, t):
                dve.wait_ge(*hhi_ready.after(KD * t + k))
                nc.vector.scalar_tensor_tensor(h_lo[:, at(k)], rows[:, at(k)], par[:, gain + k:gain + k + 1],
                                               h_hi[:, at(k)].bitcast(F32), ALU.mult, ALU.subtract).then_inc(hlo_ready.sem, 1)

            def invert(t):
                dve.wait_ge(*root_done.after(t))
                nc.vector.reciprocal(rstd[:, :], rstd[:, :]).then_inc(rstd_ready.sem, 1)

            for k in range(KD):
                h_lower(k, PAR_G, 0)
            dve.wait_ge(*w_hi_ready.after(1))
            low(w_lo[:, 1, :], w_stage[:, :], w_hi[:, 1, :]).then_inc(w_lo_ready.sem, 1)
            dve.wait_ge(act_step, 2)
            e, s_, s2, acc, z, kappa, kappa2 = (tiny[:, i, :] for i in range(7))
            link(nc.vector.tensor_scalar(s_, e, 2.0, None, ALU.add))
            link(nc.vector.reciprocal(s_, s_))
            link(nc.vector.tensor_tensor(s_, s_, e, ALU.mult))
            link(nc.vector.tensor_tensor(s2, s_, s_, ALU.mult))
            link(nc.vector.tensor_scalar(acc, s2, 1.0 / 19, 1.0 / 17, ALU.mult, ALU.add))
            for d in (15, 13, 11, 9, 7, 5, 3, 1):
                link(nc.vector.tensor_tensor(acc, acc, s2, ALU.mult))
                link(nc.vector.tensor_scalar(acc, acc, 1.0 / d, None, ALU.add))
            link(nc.vector.tensor_tensor(acc, acc, s_, ALU.mult))
            link(nc.vector.tensor_scalar(z, par[:, PAR_LAM:PAR_LAM + LT], -4.0, 0.0, ALU.mult, ALU.max))
            link(nc.vector.scalar_tensor_tensor(kappa, acc, 8.0, z, ALU.mult, ALU.add))
            nc.vector.tensor_scalar(kappa2, kappa, -2.0, None, ALU.mult).then_inc(decay_ready, 1)
            invert(0)

            def recur(J):
                th, gi, rt, a = lru_work(J)
                dve.wait_ge(*root_ready.after(J))
                link(nc.vector.scalar_tensor_tensor(a, a, 1.0, th, ALU.add, ALU.mult))
                nc.vector.tensor_tensor(gi, gi, conv[:, J % 3, :], ALU.mult)
                link(nc.vector.tensor_scalar(a, a, -1.0, 1.0, ALU.mult, ALU.add))
                link(nc.vector.scalar_tensor_tensor(rt, a, 1.0, rt, ALU.add, ALU.mult))
                link(nc.vector.tensor_tensor(rt, rt, gi, ALU.mult))
                link(nc.vector.tensor_tensor_scan(th, a, rt, 0.0, ALU.mult, ALU.add))
                dve.wait_ge(*gsilu_done.after(J))
                nc.vector.tensor_tensor(rows[:, at(J)], th, gated[:, J % 3, :], ALU.mult).then_inc(lru_done.sem, 1)

            dve.wait_ge(*scale_ready.after(0))
            dve.wait_ge(consts, 5)
            for J in range(LT):
                c = conv[:, J % 3, :]
                dve.wait_ge(*w_used.after(J * 2))
                dve.wait_ge(*conv_done.after(J - 1))
                nc.vector.tensor_tensor(taps[:, 3:3 + T], ps[0][:, :], scale[:, :], ALU.mult).then_inc(taps_ready.sem, 1)
                dve.wait_ge(*taps_ready.after(J))
                if J >= 3:
                    dve.wait_ge(*xblo_ready.after(J - 3))
                link(nc.vector.tensor_scalar(c, taps[:, 3:3 + T], par[:, PAR_CW + 3 * LT + J:PAR_CW + 3 * LT + J + 1],
                                             par[:, PAR_CB + J:PAR_CB + J + 1], ALU.mult, ALU.add))
                for tap in (2, 1, 0):
                    w = PAR_CW + tap * LT + J
                    ins = nc.vector.scalar_tensor_tensor(c, taps[:, tap:tap + T], par[:, w:w + 1], c, ALU.mult, ALU.add)
                    if tap:
                        link(ins)
                    else:
                        ins.then_inc(conv_done.sem, 1)
                if J > 1:
                    recur(J - 2)
                dve.wait_ge(*w_used.after(J * 2 + 1))
                nc.vector.tensor_tensor(gated[:, J % 3, :], ps[1][:, :], scale[:, :], ALU.mult).then_inc(gated_done.sem, 1)

            def y_low(c):
                dve.wait_ge(*yhi_act.after(c))
                hi, lo = y_col(c)
                low(split[:, lo:lo + T], rows[:, at(c)], split[:, hi:hi + T]).then_inc(ylo_dve.sem, 1)
            for c in range(GRP):
                y_low(c)
            recur(LT - 2)
            recur(LT - 1)
            y_low(LT - 1)
            dve.wait_ge(*y_split(LT - 2))
            dve.wait_ge(*y_split(LT - 1))
            for dt in range(KD):
                i, q = divmod(dt, 2)
                if dt == KD - 2:
                    for k in range(GRP):
                        h_lower(k, PAR_G + KD, 1)
                dve.wait_ge(*w_used.after(N_IN + 4 * i + 2 + q))
                dve.wait_ge(xs_loaded[q], 16 * (i + 1))
                nc.vector.tensor_tensor(rows[:, at(dt)], ps[q][:, :], work[:, q, :], ALU.add).then_inc(x1_done.sem, 1)
                if dt:
                    add_square(dt, 1)
            for k in range(GRP, KD):
                h_lower(k, PAR_G + KD, 1)

            invert(1)
            link(nc.vector.memset(fail[:, :, T:T + 1], 1.0))
            dve.wait_ge(x1_kept, 16 * KD)
            dve.wait_ge(*scale_ready.after(1))
            with dve.Fori(0, PAIRS // 2) as i:
                for m in range(2):
                    p = i * 2 + m
                    dve.wait_ge(*w_used.after(p + N_GATE))
                    nc.vector.tensor_tensor(rows[:, bass.ts(p, T)], ps[m][:, :], scale[:, :], ALU.mult).then_inc(pg_done.sem, 1)

            def scaled(n, bank=0):
                dve.wait_ge(*w_used.after(n))
                nc.vector.tensor_tensor(proj[:, :], ps[bank][:, :], scale[:, :], ALU.mult).then_inc(proj_done.sem, 1)

            def q_low(p, s):
                dve.wait_ge(*qhi_done.after(p))
                for h in range(2):
                    own, other = slice(h * HD, h * HD + HD), slice(HD - h * HD, 2 * HD - h * HD)
                    ins = low(q_pair[other, s, h, :], proj[own, :], q_pair[own, s, h, :])
                ins.then_inc(qlo_done.sem, 1)

            def k_double(p, s):
                dve.wait_ge(*khi_done.after(p))
                for h in range(2):
                    own, other = slice(h * HD, h * HD + HD), slice(HD - h * HD, 2 * HD - h * HD)
                    ins = nc.vector.tensor_copy(k_pair[other, s, h, :], k_pair[own, s, h, :].bitcast(F32))
                ins.then_inc(kdup_done.sem, 1)

            def v_low(p, s):
                for x in range(V_ROUNDS):
                    dve.wait_ge(*ahi_done.after(v_round(p) + x))
                    low(v_pair[:, s, 4 * x:4 * x + 4, :, HD:P], ps[2][:, at(v_bank(p, x), HALF)].rearrange(
                        "p (k h d) -> p k h d", k=4, h=2), v_pair[:, s, 4 * x:4 * x + 4, :, 0:HD]).then_inc(alo_done.sem, 1)

            def products(p, u):
                lo = left(u)
                dve.wait_ge(*sig_done.after(p * UNITS + u))
                keys = fail[:, u % 2, lo:T][:, ::-1]
                nc.vector.tensor_tensor_scan(keys, keys, zero[:, :].to_broadcast([P, T - lo]), 1.0, ALU.mult, ALU.add).then_inc(scan_done.sem, 1)

            def o_lower(p):
                dve.wait_ge(*ohi_ready.after(p))
                low(h_lo[:, at(p)], rows[:, at(p)], h_hi[:, at(p)]).then_inc(olo_ready.sem, 1)

            def o_join(p, k):
                h, bank = k // 4, k % 2
                own = slice(h * HD, h * HD + HD)
                v_hi = ps[3][0:HD, at(bank, HALF)].rearrange("p (u x n) -> p u x n", u=2, x=2)
                part = o_part[own, :, :]
                dve.wait_ge(*opart_done.after(p * KD + k))
                link(nc.vector.tensor_tensor(part, v_hi[:, :, 1, :], part, ALU.add))
                link(nc.vector.tensor_tensor(part, v_hi[:, :, 0, :], part, ALU.add))
                dst = rows[own, bass.ds(p * T + min(PLAN[2 * k][2], PLAN[2 * k + 1][2]) * P, 2 * P)]
                nc.vector.tensor_tensor(dst, dst, part.rearrange("p u n -> p (u n)"), ALU.mult).then_inc(o_done.sem, 1)

            def att_low(p, e, last=False):
                h, b, r, n = PLAN[e % UNITS][1:]
                for x in range(n):
                    cnt, bank, place = min(4, b + 1 - 4 * x), (r + x) % 2, PLACE[e % UNITS] + 4 * x
                    dve.wait_ge(*ahi_done.after(round_of(p, e, last) + x))
                    low(att[:, place:place + cnt, 1, :],
                        ps[2][:, bank * HALF:bank * HALF + cnt * P].rearrange("p (k n) -> p k n", k=cnt),
                        att[:, place:place + cnt, 0, :]).then_inc(alo_done.sem, 1)

            def pair(i, s, more):
                p = i * 2 + s
                for e in range(1, UNITS + 1):
                    if more and e == V_AT + 1:
                        dve.wait_ge(*klo_done.after(2 * p + 3))
                        scaled(i * 6 + 3 * s + 5 + N_QKV)
                    if e + 1 < UNITS:
                        products(p, e + 1)
                    elif more:
                        products(p + 1, e + 1 - UNITS)
                    if e < UNITS or more:
                        att_low(p, e, last=not more)
                    if e % 2 == 0:
                        o_join(p, e // 2 - 1)
                    if more and e in (Q_AT, K_AT):
                        kind = (Q_AT, K_AT).index(e)
                        if kind == 1:
                            dve.wait_ge(*qlo_done.after(p + 1))
                        scaled(i * 6 + 3 * s + 3 + kind + N_QKV)
                    if more and e == Q_AT + 2:
                        q_low(p + 1, 1 - s)
                    if more and e == K_AT + 2:
                        k_double(p + 1, 1 - s)
                    if more and e == V_TURN_AT:
                        v_low(p + 1, 1 - s)
                    for c in range(PAIRS - 1):
                        if not more and e == SPLIT_AT[c]:
                            o_lower(c)

            scaled(N_QKV)
            q_low(0, 0)
            dve.wait_ge(*qlo_done.after(0))
            scaled(N_QKV + 1, 1)
            k_double(0, 0)
            products(0, 0)
            dve.wait_ge(*klo_done.after(1))
            scaled(N_QKV + 2)
            products(0, 1)
            v_low(0, 0)
            att_low(0, 0)
            with dve.Fori(0, PAIRS // 2 - 1) as i:
                link.enter(i, 4 * KD)
                for s in range(2):
                    pair(i, s, True)
                link.leave(PAIRS // 2 - 1)
            pair(PAIRS // 2 - 1, 0, True)
            pair(PAIRS // 2 - 1, 1, False)

            o_lower(PAIRS - 1)
            dve.wait_ge(*olo_ready.after(PAIRS - 1))
            for dt in range(KD - 1):
                dve.wait_ge(*w_used.after(N_OUT2 + dt))
                dve.wait_ge(x1_loaded[dt % 2], 16 * (dt // 2 + 1))
                nc.vector.tensor_tensor(rows[:, at(dt)], ps[dt % 2][:, :], fin_x[:, dt % 2, :], ALU.add).then_inc(x2_done.sem, 1)
                if dt:
                    add_square(dt, 2)

            def last_x2(half):
                cols = at(half, HALF)
                dve.wait_ge(*half_used.after(half))
                dve.wait_ge(x1_loaded[1], 16 * (KD // 2))
                nc.vector.tensor_tensor(rows[:, (KD - 1) * T + half * HALF:(KD - 1) * T + half * HALF + HALF], ps[1][:, cols],
                                        fin_x[:, 1, cols], ALU.add).then_inc(half_x2.sem, 1)

            def last_invert(half):
                tok = slice(half * KD // 2, (half + 1) * KD // 2)
                dve.wait_ge(*root_done.after(2 + half))
                nc.vector.reciprocal(rstd[:, tok], rstd[:, tok]).then_inc(rstd_ready.sem, 1)

            def finish(half, pairs):
                cols = at(half, HALF)
                dve.wait_ge(*scale_ready.after(2 + half))
                dve.wait_ge(*gain_done.after(KD - 2))
                for k in pairs:
                    x = rows[:, 2 * k * T:2 * k * T + 2 * T].rearrange("p (k n) -> p k n", k=2)[:, :, cols]
                    rms = scale[:, cols].rearrange("p (a n) -> p a n", a=1).to_broadcast([P, 2, HALF])
                    nc.vector.tensor_tensor(fin_out[:, 2 * k:2 * k + 2, cols], x, rms, ALU.mult).then_inc(fin_dve.sem, 1)

            last_x2(0)
            last_invert(0)
            finish(0, (0,))
            last_x2(1)
            finish(0, (1, 2))
            last_invert(1)
            finish(1, (0, 1, 2))

        @block.tensor
        def _(pe):
            def sums(t):
                pe.wait_ge(*sq_added.after((KD - 1) * (t + 1) - 1))
                total = sq_buf[t][0]
                for k in range(KD):
                    ins = nc.tensor.matmul(ps[3][:, k:k + 1], total[:, at(k, P)], ones[:, :], start=True, stop=True)
                ins.then_inc(sums_done.sem, 1)

            def spread(t, blocks=range(KD)):
                pe.wait_ge(*rstd_ready.after(t))
                for k in blocks:
                    ins = nc.tensor.matmul(ps[2][:, at(k, P)], rstd[:, k:k + 1].to_broadcast([P, P]), ident[:, :],
                                           start=True, stop=True)
                ins.then_inc(rstd_spread.sem, 1)

            def tile_product(dst, wh, wl, hi, lo, first, last):
                for s in range(2):
                    cols = at(s, HALF)
                    nc.tensor.matmul(dst[:, cols], wh, split[:, hi + s * HALF:hi + s * HALF + HALF], start=first, stop=False)
                    nc.tensor.matmul(dst[:, cols], wh, split[:, lo + s * HALF:lo + s * HALF + HALF], start=False, stop=False)
                for s in range(2):
                    ins = nc.tensor.matmul(dst[:, at(s, HALF)], wl, split[:, hi + s * HALF:hi + s * HALF + HALF], start=False, stop=last)
                return ins

            def chunk(m, c, dst):
                return tile_product(dst, w_hi[:, m, at(c, P)], w_lo[:, m, at(c, P)], c * T, (KD + c) * T, c == 0, c == KD - 1)

            def project(n, m, dst, ready=None, midway=None):
                pe.wait_ge(*w_lo_ready.after(n))
                for c in range(KD):
                    if midway is not None and c in midway:
                        midway[c]()
                    if ready is not None:
                        pe.wait_ge(*ready(c))
                    ins = chunk(m, c, dst)
                ins.then_inc(w_used.sem, 1)

            def gate_products(J):
                j = J % GRP
                pe.wait_ge(*gw_lo_ready.after(J))
                pe.wait_ge(*ri_sig.after(J - 1))
                pe.wait_ge(*xblo_ready.after(J + 1 if j < GRP - 1 else J))
                slots = [s for s in range(3) if 0 <= j - 1 + s < GRP]
                for s in slots:
                    src = (J - 1 + s) % 3
                    for o in range(2):
                        w = slice(s * 256 + o * P, s * 256 + o * P + P)
                        ins = tile_product(ps[2 + o], gw_hi[:, w], gw_lo[:, w], (16 + src) * T, (19 + src) * T,
                                           s == slots[0], s == slots[-1])
                ins.then_inc(ri_done.sem, 1)

            for J in range(LT):
                pe.wait_ge(*taps_ready.after(J - 1))
                project(J * 2, 0, ps[0], hlo_ready.after if J == 0 else None)
                pe.wait_ge(*gated_done.after(J - 1))
                project(J * 2 + 1, 1, ps[1], midway={2: lambda: sums(0), 5: lambda: spread(0)} if J == 0 else None)
                if J:
                    gate_products(J - 1)
            gate_products(LT - 1)

            def y_chunk(q, c):
                return tile_product(ps[q], w_hi[:, q, at(c % GRP, P)], w_lo[:, q, at(c % GRP, P)], *y_col(c), c == 0, c == LT - 1)

            pe.wait_ge(*taps_ready.after(LT - 1))
            pe.wait_ge(*gated_done.after(LT - 1))
            for q in range(2):
                pe.wait_ge(*w_lo_ready.after(N_IN + q))
                for c in range(GRP):
                    pe.wait_ge(*y_split(c))
                    ins = y_chunk(q, c)
                ins.then_inc(w_used.sem, 1)
            for q in range(2):
                pe.wait_ge(*w_lo_ready.after(N_IN + 2 + q))
                for c in range(GRP, LT - 1):
                    pe.wait_ge(*y_split(c))
                    y_chunk(q, c)
            pe.wait_ge(*y_split(LT - 1))
            for q in range(2):
                y_chunk(q, LT - 1).then_inc(w_used.sem, 1)
            with pe.Fori(1, KD // 2) as i:
                for m in range(2):
                    for q in range(2):
                        pe.wait_ge(*w_lo_ready.after(i * 4 + 2 * m + q + N_IN))
                        if m == 0:
                            pe.wait_ge(*x1_done.after(i * 2 + q - 2))
                        for c in range(m * GRP, m * GRP + GRP):
                            ins = y_chunk(q, c)
                        ins.then_inc(w_used.sem, 1)

            pe.wait_ge(*x1_done.after(KD - 2))
            project(N_GATE, 0, ps[0], lambda c: hlo_ready.after(KD + c))
            sums(1)
            pe.wait_ge(*x1_done.after(KD - 1))
            project(N_GATE + 1, 1, ps[1], midway={KD // 2: lambda: spread(1)})
            with pe.Fori(1, PAIRS // 2) as i:
                for m in range(2):
                    pe.wait_ge(*pg_done.after(i * 2 + m - 2))
                    project(i * 2 + m + N_GATE, m, ps[m])

            def turn_v(p, x):
                if x == 0:
                    pe.wait_ge(*proj_done.after(p * 3 + 2))
                pe.wait_ge(*alo_done.after(v_round(p) + x - 2))
                for y in range(4 * x, 4 * x + 4):
                    ins = nc.tensor.transpose(ps[2][:, at(v_bank(p, x) * 4 + y % 4, P)], proj[:, at(y, P)], ident[:, :])
                ins.then_inc(turn_done.sem, 1)

            def fill(i, s, u):
                p = i * 2 + s + 1
                for x in range(sum(FILL[:u]), sum(FILL[:u + 1])):
                    kind, ch = divmod(x + FILLED, KD)
                    c = 3 * s + 3 + kind + N_QKV
                    if ch == 0:
                        pe.wait_ge(*w_lo_ready.after(i * 6 + c))
                        pe.wait_ge(*proj_done.after(p * 3 + kind - 1))
                    ins = chunk(c % 2, ch, ps[0])
                    if ch == KD - 1:
                        ins.then_inc(w_used.sem, 1)

            def scores(p, s, u):
                h, b = PLAN[u][1:3]
                lo = T - (b + 1) * P
                own, blk = slice(h * HD, h * HD + HD), at(b, P)
                if u == 0:
                    pe.wait_ge(*qlo_done.after(p))
                    pe.wait_ge(*klo_done.after(2 * p + 1))
                    pe.wait_ge(*kdup_done.after(p))
                for a, e in ((max(lo, HALF), T), (lo, HALF)):
                    if a >= e:
                        continue
                    keys = slice(a - lo, e - lo)
                    nc.tensor.matmul(ps[1][:, a:e], q_pair[:, s, h, blk], k_pair[:, s, h, keys], start=True, stop=False)
                    ins = nc.tensor.matmul(ps[1][:, a:e], q_pair[own, s, h, blk], k_low[own, s, keys], start=False, stop=e < T)
                    if e == T:
                        ins = nc.tensor.matmul(ps[1][:, T - P:T], ident_b[:, :], mask[:, :], start=False, stop=True)
                ins.then_inc(z_ready.sem, 1)

            def turn(p, u, last=False):
                h, b, r, n = PLAN[u][1:]
                pe.wait_ge(*att_done.after(p * UNITS + u))
                lo = left(u)
                for x in range(n):
                    bank = (r + x) % 2
                    pe.wait_ge(*alo_done.after(round_of(p, u, last) + x - 2))
                    for y in range(4 * x, min(4 * x + 4, b + 1)):
                        ins = nc.tensor.transpose(ps[2][:, bank * HALF + (y % 4) * P:bank * HALF + (y % 4) * P + P],
                                                  beta[:, u % 2, lo + y * P:lo + y * P + P], ident[:, :])
                    ins.then_inc(turn_done.sem, 1)

            def values(p, s, u, last=False):
                h, b, r, n = PLAN[u][1:]
                bank = (u // 2) % 2
                if u % 2 == 0:
                    pe.wait_ge(*o_done.after(p * KD + u // 2 - 2))
                col = bank * HALF + (b % 2) * 2 * P
                for x in range(n):
                    pe.wait_ge(*alo_done.after(round_of(p, u, last) + x))
                    for y in range(4 * x, min(4 * x + 4, b + 1)):
                        ins = nc.tensor.matmul(ps[3][:, col:col + 2 * P], v_pair[:, s, y, h, :],
                                               att[:, PLACE[u] + y, :, :].rearrange("p x n -> p (x n)"), start=y == 0, stop=y == b)
                ins.then_inc(av_done.sem, 1)

            def prepare(p, s, e, more):
                if e < UNITS:
                    turn(p, e, not more)
                elif more:
                    turn(p + 1, 0)
                if e + 2 < UNITS or more:
                    pe.wait_ge(*sig_done.after(p * UNITS + e + 1))
                    if e + 2 < UNITS:
                        scores(p, s, e + 2)
                    else:
                        scores(p + 1, 1 - s, e + 2 - UNITS)

            def pair(i, s, more):
                p = i * 2 + s
                for u in range(UNITS):
                    early = (u + 1) % UNITS in EARLY
                    if more and u == V_TURN_AT:
                        turn_v(p + 1, 0)
                    if more and (u < AHEAD or more == "all"):
                        fill(i, s, u)
                    if more and u == V_TURN_AT:
                        turn_v(p + 1, 1)
                    if not more and u in OUT_AT:
                        if u == OUT_AT[0]:
                            pe.wait_ge(*w_lo_ready.after(N_OUT2))
                            pe.wait_ge(*proj_done.after(3 * PAIRS - 1))
                        pe.wait_ge(*olo_ready.after(OUT_AT.index(u)))
                        chunk(0, OUT_AT.index(u), ps[0])
                    if not more and u == UNITS - 1:
                        pe.wait_ge(*w_lo_ready.after(N_OUT2 + 1))
                        pe.wait_ge(*sig_done.after(p * UNITS + UNITS - 1))
                        chunk(1, 0, ps[1])
                    if early:
                        prepare(p, s, u + 1, more)
                    values(p, s, u, not more)
                    if not early:
                        prepare(p, s, u + 1, more)

            pe.wait_ge(*pg_done.after(PAIRS - 2))
            project(N_QKV, 0, ps[0])
            pe.wait_ge(*pg_done.after(PAIRS - 1))
            project(N_QKV + 1, 1, ps[1])
            pe.wait_ge(*proj_done.after(0))
            project(N_QKV + 2, 0, ps[0], midway={KD - 1: lambda: scores(0, 0, 0)})
            pe.wait_ge(*sig_done.after(0))
            scores(0, 0, 1)
            for x in range(V_ROUNDS):
                turn_v(0, x)
            pe.wait_ge(*w_lo_ready.after(N_QKV + 3))
            for c in range(FILLED):
                chunk(1, c, ps[0])
            prepare(0, 0, 0, True)
            with pe.Fori(0, PAIRS // 2 - 1) as i:
                for s in range(2):
                    pair(i, s, "all")
            pair(PAIRS // 2 - 1, 0, True)
            pair(PAIRS // 2 - 1, 1, False)

            for c in range(1, KD - 1):
                chunk(1, c, ps[1])
            pe.wait_ge(*olo_ready.after(PAIRS - 1))
            for m in range(2):
                chunk(m, KD - 1, ps[m]).then_inc(w_used.sem, 1)
            with pe.Fori(1, KD // 2 - 1) as i:
                for q in range(2):
                    pe.wait_ge(*x2_done.after(i * 2 + q - 2))
                    project(i * 2 + q + N_OUT2, q, ps[q])
            pe.wait_ge(*x2_done.after(KD - 4))
            project(N_ALL - 2, 0, ps[0])

            def half_sums(half):
                pe.wait_ge(*sq_added.after(3 * KD - 5))
                pe.wait_ge(*half_sq.after(half))
                for k in range(half * KD // 2, (half + 1) * KD // 2):
                    nc.tensor.matmul(ps[3][:, k:k + 1], fin_sum[:, at(k, P)], ones[:, :], start=True, stop=False)
                    ins = nc.tensor.matmul(ps[3][:, k:k + 1], fin_sq[:, 1, at(k, P)], ones[:, :], start=False, stop=True)
                ins.then_inc(sums_done.sem, 1)

            pe.wait_ge(*x2_done.after(KD - 3))
            pe.wait_ge(*w_lo_ready.after(N_ALL - 1))
            for half in range(2):
                cols = at(half, HALF)
                for c in range(KD):
                    if half == 1 and c == 3:
                        half_sums(0)
                    if half == 1 and c == 6:
                        spread(2, range(KD // 2))
                    m_hi = h_hi[:, c * T + half * HALF:c * T + half * HALF + HALF]
                    m_lo = h_lo[:, c * T + half * HALF:c * T + half * HALF + HALF]
                    nc.tensor.matmul(ps[1][:, cols], w_hi[:, 1, at(c, P)], m_hi, start=c == 0, stop=False)
                    nc.tensor.matmul(ps[1][:, cols], w_hi[:, 1, at(c, P)], m_lo, start=False, stop=False)
                    ins = nc.tensor.matmul(ps[1][:, cols], w_lo[:, 1, at(c, P)], m_hi, start=False, stop=c == KD - 1)
                ins.then_inc(half_used.sem, 1)
            half_sums(1)
            spread(3, range(KD // 2, KD))


def kernel(**inputs):
    import numpy as np
    import concourse.bacc as bacc
    from concourse.bass_utils import run_bass_kernel_spmd

    a = {k: np.asarray(v) for k, v in inputs.items()}

    def cols(v):
        return v.reshape(-1, P).T

    heads, blk = a["lru_w_gates"].shape[1], a["lru_w_gates"].shape[2]
    bg = a["lru_b_gates"][0]
    params = np.concatenate(
        [cols(a["norm_g"][0]), cols(a["norm_g"][1])] + [cols(a["lru_conv_w"][0, t]) for t in range(4)]
        + [cols(a["lru_conv_b"][0]), cols(np.ascontiguousarray(bg[:, :blk]).reshape(-1)),
           cols(np.ascontiguousarray(bg[:, blk:]).reshape(-1)), cols(a["lru_lambda"][0]), cols(a["final_norm_g"])], axis=1)
    full = np.zeros((2, LRU, LRU), np.float32)
    for h in range(heads):
        s = slice(h * blk, h * blk + blk)
        full[0, s, s] = a["lru_w_gates"][0, h, :, :blk]
        full[1, s, s] = a["lru_w_gates"][0, h, :, blk:]
    w_gate = np.zeros((LT, P, 3, 2, P), np.float32)
    for t in range(LT):
        for s in range(3):
            if 0 <= t - 1 + s < LT:
                w_gate[t, :, s] = full[:, (t - 1 + s) * P:(t + s) * P, t * P:(t + 1) * P].transpose(1, 0, 2)
    w_gate = w_gate.reshape(LT, P, 3 * 256)

    def tiles(w, chunks):
        k, n = w.shape
        return w.reshape(k // (P * chunks), chunks, P, n // P, P).transpose(3, 0, 2, 1, 4).reshape(n // P, -1, P, chunks * P)

    wi = tiles(a["lru_w_in"][0], KD)[:, 0]
    wi = np.stack([wi[:LT], wi[LT:]], axis=1).reshape(N_IN, P, D)
    wo = tiles(a["lru_w_out"][0], GRP).reshape(KD // 2, 2, 2, P, GRP * P).transpose(0, 2, 1, 3, 4).reshape(2 * KD, P, GRP * P)
    wo = np.concatenate([wo, np.zeros((2 * KD, P, D - GRP * P), np.float32)], axis=2)
    sbw = tiles(a["sb_w_in"][0], KD)[:, 0].reshape(4, KD, P, D).transpose(1, 0, 2, 3).reshape(4 * KD, P, D)
    sbo = tiles(a["sb_w_out"][0], KD)[:, 0]
    weights = np.concatenate([wi, wo, sbw[3::4], sbw.reshape(KD, 4, P, D)[:, :3].reshape(3 * KD, P, D), sbo], axis=0)
    host = {"xT": np.ascontiguousarray(a["x"][0].T).reshape(KD, P, T), "params": params, "weights": weights, "w_gate": w_gate}

    nc = bacc.Bacc("TRN2", target_bir_lowering=False, num_devices=1)
    arrays, args = {}, []
    for name, v in host.items():
        v = np.ascontiguousarray(v)
        arrays[f"in_{name}"] = v
        args.append(nc.dram_tensor(f"in_{name}", v.shape, mybir.dt.from_np(v.dtype), kind="ExternalInput").ap())
    out = nc.dram_tensor("out_dram", (KD, P, T), mybir.dt.float32, kind="ExternalOutput").ap()
    kept = nc.dram_tensor("kept_x1", (KD, P, T), mybir.dt.float32, kind="Internal").ap()
    build(nc, *args, kept, out)
    r = run_bass_kernel_spmd(nc, [arrays], core_ids=[0])
    return r.results[0]["out_dram"].reshape(D, T).T.reshape(1, T, D)
```
